# Optimizing a Trainium2 kernel written in Bass

```python
import math
import jax, jax.numpy as jnp
from jax import lax
import numpy as np

D_MODEL = 1024
BATCH = 1
SEQ = 256
DEPTH = 1

PLE_DIM = 256
EPS = 1e-6
GLA_HEADS = 4
GLA_DK = D_MODEL // 2 // GLA_HEADS
GLA_DV = D_MODEL // GLA_HEADS
GLA_RANK = 16
GLA_TAU = 16.0
GLA_CHUNK = 64
GLA_QK_W = GLA_HEADS * GLA_DK
GLA_V_W = GLA_HEADS * GLA_DV
ATT_GROUPS = ((128, 1), (512, 4), (2048, 16))
ATT_HEADS_PER_GROUP = 4
ATT_HEAD_DIM = 128
N_ATT_GROUPS = len(ATT_GROUPS)
N_ATT_HEADS = N_ATT_GROUPS * ATT_HEADS_PER_GROUP
ATT_W = ATT_HEADS_PER_GROUP * ATT_HEAD_DIM
ATT_BLOCK = 128
REL_BUCKETS = 32
REL_MAX_DIST = 2048
D_FF = 4 * D_MODEL
NEG_INF = -1e30

SPLIT_SIZES = (GLA_QK_W, GLA_QK_W, GLA_V_W, GLA_V_W, GLA_RANK,
               N_ATT_GROUPS * 3 * ATT_W, 2 * D_MODEL)
IN_COLS = sum(SPLIT_SIZES)


def rmsnorm(x, g):
    xf = x.astype(jnp.float32)
    y = xf * lax.rsqrt(jnp.mean(xf * xf, axis=-1, keepdims=True) + EPS)
    return (y * g.astype(jnp.float32)).astype(x.dtype)

def _split_cols(h, sizes):
    offsets = np.cumsum(np.array(sizes))[:-1].tolist()
    return jnp.split(h, offsets, axis=-1)

def _t5_causal_bucket(n):
    max_exact = REL_BUCKETS // 2
    nf = np.maximum(n, 1).astype(np.float32)
    large = max_exact + (np.log(nf / max_exact) / np.log(REL_MAX_DIST / max_exact)
                         * (REL_BUCKETS - max_exact)).astype(np.int32)
    large = np.minimum(large, REL_BUCKETS - 1)
    return np.where(n < max_exact, n, large).astype(np.int32)

def _group_bias(rel_bias, g, dil):
    qi = np.arange(ATT_BLOCK)[:, None]
    kj = np.arange(2 * ATT_BLOCK)[None, :]
    dist = np.maximum(qi + ATT_BLOCK - kj, 0) * dil
    bucket = _t5_causal_bucket(dist)
    tab = rel_bias[:, g * ATT_HEADS_PER_GROUP:(g + 1) * ATT_HEADS_PER_GROUP]
    return jnp.transpose(tab[bucket], (2, 0, 1)).astype(jnp.float32)

def gla_mixer(q, k, v, log_a):
    B, S, H, dk = q.shape
    dv = v.shape[-1]
    C = GLA_CHUNK
    N = S // C

    def chunk(t):
        return t.astype(jnp.float32).reshape(B, N, C, H, t.shape[-1]).transpose(0, 3, 1, 2, 4)

    q, k, v, g = chunk(q), chunk(k), chunk(v), chunk(log_a)
    b = jnp.cumsum(g, axis=3)
    b_last = b[:, :, :, -1:, :]
    q_dec = q * (dk ** -0.5) * jnp.exp(b)
    k_in = k * jnp.exp(-b)
    k_out = k * jnp.exp(b_last - b)
    causal = np.tril(np.ones((C, C), dtype=bool))
    attn = jnp.where(causal, jnp.einsum('bhncd,bhnsd->bhncs', q_dec, k_in), 0.0)
    o_intra = jnp.einsum('bhncs,bhnsv->bhncv', attn, v)
    upd = jnp.einsum('bhncd,bhncv->nbhdv', k_out, v)
    decay = jnp.exp(b_last[:, :, :, 0, :]).transpose(2, 0, 1, 3)

    def step(state, inp):
        dec, u = inp
        return dec[..., None] * state + u, state

    _, states = lax.scan(step, jnp.zeros((B, H, dk, dv), jnp.float32), (decay, upd))
    o_inter = jnp.einsum('bhncd,nbhdv->bhncv', q_dec, states)
    return (o_intra + o_inter).transpose(0, 2, 3, 1, 4).reshape(B, S, H, dv)

def dilated_attention(q, k, v, bias, dil, win_steps):
    B, S, H, hd = q.shape
    BLK = ATT_BLOCK
    L = S // dil
    nb = -(-L // BLK)
    Lp = nb * BLK
    Z = B * dil

    def sub(t):
        return t.reshape(B, L, dil, H, hd).transpose(0, 2, 3, 1, 4).reshape(Z, H, L, hd)

    qs = jnp.pad(sub(q), ((0, 0), (0, 0), (0, Lp - L), (0, 0))).reshape(Z, H, nb, BLK, hd)

    def kv_blocks(t):
        t = jnp.pad(sub(t), ((0, 0), (0, 0), (BLK, Lp - L), (0, 0))).reshape(Z, H, nb + 1, BLK, hd)
        return jnp.concatenate([t[:, :, :-1], t[:, :, 1:]], axis=3)

    kb, vb = kv_blocks(k), kv_blocks(v)
    qi = np.arange(BLK)[:, None]
    kj = np.arange(2 * BLK)[None, :]
    delta = qi + BLK - kj
    band = (delta >= 0) & (delta <= win_steps)
    valid = band[None] & ((np.arange(nb)[:, None, None] > 0) | (kj >= BLK)[None])
    logits = jnp.einsum('zhnqd,zhnkd->zhnqk', qs, kb).astype(jnp.float32) * (hd ** -0.5)
    logits = jnp.where(valid, logits + bias[:, None], NEG_INF)
    m = jnp.max(logits, axis=-1, keepdims=True)
    pexp = jnp.exp(logits - m)
    s = jnp.sum(pexp, axis=-1, keepdims=True)
    o = jnp.einsum('zhnqk,zhnkd->zhnqd', pexp, vb.astype(jnp.float32)) / s
    lse = (m + jnp.log(s))[..., 0]
    o = o.reshape(B, dil, H, Lp, hd)[:, :, :, :L].transpose(0, 3, 1, 2, 4).reshape(B, S, H, hd)
    lse = lse.reshape(B, dil, H, Lp)[..., :L].transpose(0, 3, 1, 2).reshape(B, S, H)
    return o, lse

def first_inputs(seed: int = 0) -> dict:
    key = jax.random.key(seed)
    ks = jax.random.split(key, 20)

    def nrm(k, shape, scale):
        return jax.random.normal(k, shape, jnp.float32) * scale

    return {
        "x": nrm(ks[0], (BATCH, SEQ, D_MODEL), 1.0),
        "p": nrm(ks[1], (DEPTH, BATCH, SEQ, PLE_DIM), 1.0),
        "ln1": 1.0 + nrm(ks[2], (DEPTH, D_MODEL), 0.02),
        "w_in": nrm(ks[3], (DEPTH, D_MODEL, IN_COLS), D_MODEL ** -0.5),
        "w_a2": nrm(ks[4], (DEPTH, GLA_RANK, GLA_QK_W), GLA_RANK ** -0.5),
        "b_a": nrm(ks[5], (DEPTH, GLA_QK_W), 0.1),
        "gla_gn": 1.0 + nrm(ks[6], (DEPTH, GLA_V_W), 0.02),
        "w_o_gla": nrm(ks[7], (DEPTH, GLA_V_W, D_MODEL), GLA_V_W ** -0.5),
        "w_o_attn": nrm(ks[8], (DEPTH, ATT_W, D_MODEL), ATT_W ** -0.5),
        "w_out": nrm(ks[9], (DEPTH, D_MODEL, D_MODEL), D_MODEL ** -0.5),
        "ln2": 1.0 + nrm(ks[10], (DEPTH, D_MODEL), 0.02),
        "w_mlp1": nrm(ks[11], (DEPTH, D_MODEL, D_FF), D_MODEL ** -0.5),
        "w_mlp2": nrm(ks[12], (DEPTH, D_FF, D_MODEL), D_FF ** -0.5),
        "ln3": 1.0 + nrm(ks[13], (DEPTH, D_MODEL), 0.02),
        "w_pp": nrm(ks[14], (DEPTH, PLE_DIM, D_MODEL), PLE_DIM ** -0.5),
        "w_pg": nrm(ks[15], (DEPTH, D_MODEL, D_MODEL), D_MODEL ** -0.5),
        "rel_bias": nrm(ks[16], (REL_BUCKETS, N_ATT_HEADS), 0.5),
        "ln_f": 1.0 + nrm(ks[17], (D_MODEL,), 0.02),
    }

def first_block(x, p, ln1, w_in, w_a2, b_a, gla_gn, w_o_gla, w_o_attn, w_out,
              ln2, w_mlp1, w_mlp2, ln3, w_pp, w_pg, rel_bias, ln_f):
    B, S, _ = x.shape
    for i in range(DEPTH):
        h = rmsnorm(x, ln1[i])
        hq, hk, hv, hr, ha, hatt, hgate = _split_cols(h @ w_in[i], SPLIT_SIZES)

        log_a = jax.nn.log_sigmoid((ha @ w_a2[i] + b_a[i]).astype(jnp.float32)) / GLA_TAU
        o = gla_mixer(hq.reshape(B, S, GLA_HEADS, GLA_DK),
                      hk.reshape(B, S, GLA_HEADS, GLA_DK),
                      hv.reshape(B, S, GLA_HEADS, GLA_DV),
                      log_a.reshape(B, S, GLA_HEADS, GLA_DK))
        o = o * lax.rsqrt(jnp.mean(o * o, axis=-1, keepdims=True) + EPS)
        o = o.reshape(B, S, GLA_V_W) * gla_gn[i].astype(jnp.float32) * jax.nn.silu(hr.astype(jnp.float32))
        y_gla = o.astype(x.dtype) @ w_o_gla[i]

        hatt = hatt.reshape(B, S, N_ATT_GROUPS, 3, ATT_HEADS_PER_GROUP, ATT_HEAD_DIM)
        outs, lses = [], []
        for g, (win, dil) in enumerate(ATT_GROUPS):
            o_g, lse_g = dilated_attention(hatt[:, :, g, 0], hatt[:, :, g, 1], hatt[:, :, g, 2],
                                           _group_bias(rel_bias, g, dil), dil, win // dil)
            outs.append(o_g)
            lses.append(lse_g)
        wts = jax.nn.softmax(jnp.stack(lses, axis=0), axis=0)
        o_att = jnp.sum(wts[..., None] * jnp.stack(outs, axis=0), axis=0).reshape(B, S, ATT_W)
        y_att = o_att.astype(x.dtype) @ w_o_attn[i]

        g_gla, g_att = jnp.split(hgate, 2, axis=-1)
        mix = (jax.nn.sigmoid(g_gla) * y_gla + jax.nn.sigmoid(g_att) * y_att) @ w_out[i]
        x = x + mix

        h2 = rmsnorm(x, ln2[i])
        x = x + jnp.square(jax.nn.relu(h2 @ w_mlp1[i])) @ w_mlp2[i]

        h3 = rmsnorm(x, ln3[i])
        x = x + jax.nn.sigmoid(h3 @ w_pg[i]) * (p[i] @ w_pp[i])
    return rmsnorm(x, ln_f)


DEPTH_2 = 2

CHUNK = 64
N_MIXERS = 2
N_CONV_LAYERS = (DEPTH_2 + 1) // 2
N_MLA_LAYERS = DEPTH_2 // 2
D_FF_2 = 2816
FFN_RES_WEIGHT = 0.5
CONV_WIDTH = 31
N_HEADS = 8
QK_NOPE = 128
QK_ROPE = 64
V_HEAD = 128
Q_LORA = 512
KV_LORA = 256
ROPE_THETA = 10000.0
Q_BLOCK = 128
RMS_EPS = 1e-6
POS_OFFSET_MAX = 65536


def rmsnorm_2(x, g):
    xf = x.astype(jnp.float32)
    y = xf * lax.rsqrt(jnp.mean(xf * xf, axis=-1, keepdims=True) + RMS_EPS) * g.astype(jnp.float32)
    return y.astype(x.dtype)

def swiglu_ffn(h, w1, w3, w2):
    return (jax.nn.silu(h @ w1) * (h @ w3)) @ w2

def conv_module(h, w_pw1, w_dw, g_norm, w_pw2):
    u = h @ w_pw1
    a, b = jnp.split(u, 2, axis=-1)
    u = a * jax.nn.sigmoid(b)
    u = lax.conv_general_dilated(
        u, w_dw[:, None, :].astype(u.dtype), window_strides=(1,),
        padding=[(CONV_WIDTH - 1, 0)],
        dimension_numbers=("NWC", "WIO", "NWC"),
        feature_group_count=D_MODEL)
    u = jax.nn.silu(rmsnorm_2(u, g_norm))
    return u @ w_pw2

def apply_rope(x, cos, sin):
    half = x.shape[-1] // 2
    xf = x.astype(jnp.float32)
    x1, x2 = xf[..., :half], xf[..., half:]
    out = jnp.concatenate([x1 * cos - x2 * sin, x2 * cos + x1 * sin], axis=-1)
    return out.astype(x.dtype)

def mla(h, positions, w_a, g_q, g_kv, w_uq, w_ukv, w_o):
    a = h @ w_a
    c_q = rmsnorm_2(a[..., :Q_LORA], g_q)
    c_kv = rmsnorm_2(a[..., Q_LORA:Q_LORA + KV_LORA], g_kv)
    k_rope = a[..., Q_LORA + KV_LORA:]
    q = jnp.einsum("bsc,chd->bshd", c_q, w_uq)
    q_nope, q_rope = q[..., :QK_NOPE], q[..., QK_NOPE:]
    kv = jnp.einsum("bsc,chd->bshd", c_kv, w_ukv)
    k_nope, v = kv[..., :QK_NOPE], kv[..., QK_NOPE:]

    inv_freq = ROPE_THETA ** (-2.0 * jnp.arange(QK_ROPE // 2, dtype=jnp.float32) / QK_ROPE)
    ang = positions.astype(jnp.float32)[..., None] * inv_freq
    cos, sin = jnp.cos(ang), jnp.sin(ang)
    q_rope = apply_rope(q_rope, cos[:, :, None, :], sin[:, :, None, :])
    k_rope = apply_rope(k_rope, cos, sin)

    seq = h.shape[1]
    scale = (QK_NOPE + QK_ROPE) ** -0.5
    chunk_id = jnp.arange(seq) // CHUNK
    outs = []
    for blk in range(seq // Q_BLOCK):
        q0, q1 = blk * Q_BLOCK, (blk + 1) * Q_BLOCK
        s = (jnp.einsum("bqhd,bkhd->bhqk", q_nope[:, q0:q1], k_nope[:, :q1],
                        preferred_element_type=jnp.float32)
             + jnp.einsum("bqhr,bkr->bhqk", q_rope[:, q0:q1], k_rope[:, :q1],
                          preferred_element_type=jnp.float32)) * scale
        mask = chunk_id[q0:q1, None] >= chunk_id[None, :q1]
        s = jnp.where(mask[None, None], s, -jnp.inf)
        p = jax.nn.softmax(s, axis=-1).astype(v.dtype)
        outs.append(jnp.einsum("bhqk,bkhd->bqhd", p, v[:, :q1]))
    o = jnp.concatenate(outs, axis=1)
    return o.reshape(o.shape[0], seq, N_HEADS * V_HEAD) @ w_o

def second_inputs(seed: int = 0) -> dict:
    key = jax.random.key(seed)
    ks = jax.random.split(key, 24)
    f32 = jnp.float32

    def w(k, shape, fan_in):
        return jax.random.normal(k, shape, f32) * (fan_in ** -0.5)

    def gain(k, shape):
        return 1.0 + 0.02 * jax.random.normal(k, shape, f32)

    x = jax.random.normal(ks[0], (BATCH, SEQ, D_MODEL), f32)
    offset = jax.random.randint(ks[1], (BATCH, 1), 0, POS_OFFSET_MAX, dtype=jnp.int32)
    positions = offset + jnp.arange(SEQ, dtype=jnp.int32)[None, :]
    return {
        "x": x,
        "positions": positions,
        "ffn_norm1": gain(ks[2], (DEPTH_2, D_MODEL)),
        "ffn1_w1": w(ks[3], (DEPTH_2, D_MODEL, D_FF_2), D_MODEL),
        "ffn1_w3": w(ks[4], (DEPTH_2, D_MODEL, D_FF_2), D_MODEL),
        "ffn1_w2": w(ks[5], (DEPTH_2, D_FF_2, D_MODEL), D_FF_2),
        "mix_norm": gain(ks[6], (DEPTH_2, D_MODEL)),
        "ffn_norm2": gain(ks[7], (DEPTH_2, D_MODEL)),
        "ffn2_w1": w(ks[8], (DEPTH_2, D_MODEL, D_FF_2), D_MODEL),
        "ffn2_w3": w(ks[9], (DEPTH_2, D_MODEL, D_FF_2), D_MODEL),
        "ffn2_w2": w(ks[10], (DEPTH_2, D_FF_2, D_MODEL), D_FF_2),
        "conv_w_pw1": w(ks[11], (N_CONV_LAYERS, D_MODEL, 2 * D_MODEL), D_MODEL),
        "conv_w_dw": w(ks[12], (N_CONV_LAYERS, CONV_WIDTH, D_MODEL), CONV_WIDTH),
        "conv_norm": gain(ks[13], (N_CONV_LAYERS, D_MODEL)),
        "conv_w_pw2": w(ks[14], (N_CONV_LAYERS, D_MODEL, D_MODEL), D_MODEL),
        "mla_w_a": w(ks[15], (N_MLA_LAYERS, D_MODEL, Q_LORA + KV_LORA + QK_ROPE), D_MODEL),
        "mla_q_norm": gain(ks[16], (N_MLA_LAYERS, Q_LORA)),
        "mla_kv_norm": gain(ks[17], (N_MLA_LAYERS, KV_LORA)),
        "mla_w_uq": w(ks[18], (N_MLA_LAYERS, Q_LORA, N_HEADS, QK_NOPE + QK_ROPE), Q_LORA),
        "mla_w_ukv": w(ks[19], (N_MLA_LAYERS, KV_LORA, N_HEADS, QK_NOPE + V_HEAD), KV_LORA),
        "mla_w_o": w(ks[20], (N_MLA_LAYERS, N_HEADS * V_HEAD, D_MODEL), N_HEADS * V_HEAD),
        "final_norm": gain(ks[21], (D_MODEL,)),
    }

def second_block(x, positions, ffn_norm1, ffn1_w1, ffn1_w3, ffn1_w2, mix_norm, ffn_norm2,
              ffn2_w1, ffn2_w3, ffn2_w2, conv_w_pw1, conv_w_dw, conv_norm, conv_w_pw2,
              mla_w_a, mla_q_norm, mla_kv_norm, mla_w_uq, mla_w_ukv, mla_w_o, final_norm):
    h = x
    for i in range(DEPTH_2):
        h = h + FFN_RES_WEIGHT * swiglu_ffn(rmsnorm_2(h, ffn_norm1[i]), ffn1_w1[i], ffn1_w3[i], ffn1_w2[i])
        m = rmsnorm_2(h, mix_norm[i])
        j = i // N_MIXERS
        if i % N_MIXERS == 0:
            h = h + conv_module(m, conv_w_pw1[j], conv_w_dw[j], conv_norm[j], conv_w_pw2[j])
        else:
            h = h + mla(m, positions, mla_w_a[j], mla_q_norm[j], mla_kv_norm[j],
                        mla_w_uq[j], mla_w_ukv[j], mla_w_o[j])
        h = h + FFN_RES_WEIGHT * swiglu_ffn(rmsnorm_2(h, ffn_norm2[i]), ffn2_w1[i], ffn2_w3[i], ffn2_w2[i])
    return rmsnorm_2(h, final_norm)


def setup_inputs(seed=0):
    out = dict(first_inputs(seed))
    for name, value in second_inputs(seed + 1).items():
        if name != "x":
            out[name + "_2"] = value
    return out


def reference(
    x, p, ln1, w_in, w_a2, b_a, gla_gn, w_o_gla, w_o_attn, w_out, ln2, w_mlp1, w_mlp2, ln3,
    w_pp, w_pg, rel_bias, ln_f, positions_2, ffn_norm1_2, ffn1_w1_2, ffn1_w3_2, ffn1_w2_2,
    mix_norm_2, ffn_norm2_2, ffn2_w1_2, ffn2_w3_2, ffn2_w2_2, conv_w_pw1_2, conv_w_dw_2,
    conv_norm_2, conv_w_pw2_2, mla_w_a_2, mla_q_norm_2, mla_kv_norm_2, mla_w_uq_2, mla_w_ukv_2,
    mla_w_o_2, final_norm_2,
):
    x = first_block(
        x, p, ln1, w_in, w_a2, b_a, gla_gn, w_o_gla, w_o_attn, w_out, ln2, w_mlp1, w_mlp2, ln3,
        w_pp, w_pg, rel_bias, ln_f,
    )
    return second_block(
        x, positions_2, ffn_norm1_2, ffn1_w1_2, ffn1_w3_2, ffn1_w2_2, mix_norm_2, ffn_norm2_2,
        ffn2_w1_2, ffn2_w3_2, ffn2_w2_2, conv_w_pw1_2, conv_w_dw_2, conv_norm_2, conv_w_pw2_2,
        mla_w_a_2, mla_q_norm_2, mla_kv_norm_2, mla_w_uq_2, mla_w_ukv_2, mla_w_o_2,
        final_norm_2,
    )


_drawn_inputs = setup_inputs


def setup_inputs(seed=0):
    import zlib

    import numpy as np

    out = dict(_drawn_inputs(seed))
    spreads = {}
    factors = {'ln1': 3.483,
     'b_a': 3.555,
     'gla_gn': 7.559,
     'ln2': 3.054,
     'ln3': 54.508,
     'ffn_norm1_2': 5.117,
     'mix_norm_2': 4.343,
     'ffn_norm2_2': 5.973,
     'conv_norm_2': 4.15,
     'mla_q_norm_2': 8.0,
     'mla_kv_norm_2': 8.0,
     'final_norm_2': 8.084}
    for name, (base, spread) in spreads.items():
        noise = np.random.default_rng([zlib.crc32(name.encode()), seed]).standard_normal(out[name].shape)
        drawn = base * np.exp(spread * noise) if base else spread * noise
        out[name] = __import__('jax').numpy.asarray(drawn.astype(out[name].dtype))
    for name, factor in factors.items():
        out[name] = (out[name] * factor).astype(out[name].dtype)
    return out
```

```python
from contextlib import ExitStack

import numpy as np

import concourse.bass as bass
from concourse import mybir

F32 = mybir.dt.float32
F32R = mybir.dt.float32r
I32 = mybir.dt.int32
ACT = mybir.ActivationFunctionType
ALU = mybir.AluOpType
AX_X = mybir.AxisListType.X

P = 128
D = 1024
T = 256
NT = T // P
NC = D // P
EPS = 1e-6
W = 256
RAW = 4
RING = 8
AHEAD = 5
PLE = 256
GLA_H, GLA_DK, GLA_DV, GLA_RANK, GLA_CHUNK = 4, 128, 256, 16, 64
GLA_QK, GLA_V = GLA_H * GLA_DK, GLA_H * GLA_DV
ATT_GROUPS = ((128, 1), (512, 4), (2048, 16))
ATT_G, ATT_H, HD = 3, 4, 128
ATT_W = ATT_H * HD
REL_BUCKETS, REL_MAX_DIST = 32, 2048
NEG = -1e30
FF1, FF2 = 4 * D, 2816
CONV_W = 31
MLA_H, NOPE, ROPE, VH, Q_LORA, KV_LORA = 8, 128, 64, 128, 512, 256
MLA_CHUNK = 64
ROPE_THETA = 10000.0
BIAS_N = 384

COL_HA = 2 * GLA_QK + 2 * GLA_V
COL_ATT = COL_HA + GLA_RANK
COL_GATE = COL_ATT + ATT_G * 3 * ATT_W

GAINS = (("ln1", 8), ("ln2", 8), ("ln3", 8), ("gla_gn", 8), ("ln_f", 8), ("ffn_norm1_2", 16),
         ("mix_norm_2", 16), ("ffn_norm2_2", 16), ("conv_norm_2", 8), ("mla_q_norm_2", 4),
         ("mla_kv_norm_2", 2), ("final_norm_2", 8))
GAIN_AT, _n = {}, 0
for _name, _c in GAINS:
    GAIN_AT[_name] = _n
    _n += _c
GAIN_N = _n


def bias_table():
    out = np.zeros((REL_BUCKETS + 1, ATT_G, BIAS_N), np.float32)
    exact = REL_BUCKETS // 2
    for g, (win, dil) in enumerate(ATT_GROUPS):
        for j in range(BIAS_N):
            dist = 255 - j
            if dist < 0 or dist > win or dist % dil:
                out[REL_BUCKETS, g, j] = NEG
                continue
            nf = np.float32(max(dist, 1))
            large = exact + int(np.float32(np.log(nf / np.float32(exact)) / np.float32(np.log(REL_MAX_DIST / exact))
                                           * np.float32(REL_BUCKETS - exact)))
            out[dist if dist < exact else min(large, REL_BUCKETS - 1), g, j] = 1.0
    return out


def rope_table():
    half = ROPE // 2
    freq = (ROPE_THETA ** (-2.0 * np.arange(half) / ROPE)).astype(np.float32)
    out = np.zeros((P, 1 + P), np.float32)
    for m in range(P):
        out[m, 0] = freq[m % half]
        if m % ROPE < half:
            out[m + half, 1 + m] = -1.0
        else:
            out[m - half, 1 + m] = 1.0
    return out


def lin(const, coeff, i):
    return const if i is None or coeff == 0 else i * coeff + const


class Phase:

    def __init__(self, name, src, groups, kns, moving, evac, layout="F", width=W, loop=None):
        self.name, self.src, self.groups, self.kns = name, src, groups, kns
        self.moving, self.evac, self.layout, self.width, self.loop = moving, evac, layout, width, loop
        self.k0 = [sum(kns[:j]) for j in range(len(kns))]

    def segments(self):
        if self.loop is None:
            yield list(range(self.groups)), None
            return
        first, per, turns = self.loop
        yield list(range(first)), None
        yield list(range(first, first + per)), turns
        yield list(range(first + per * turns, self.groups)), None

    def block(self, g, j):
        return self.block0 + g * len(self.kns) + j


def program(nc, a, out):
    with ExitStack() as ctx:
        def sb(name, shape, dt=F32):
            return ctx.enter_context(nc.sbuf_tensor(name, shape, dt))

        def sem(name):
            return ctx.enter_context(nc.semaphore(name))

        guard = nc.sbuf_tensor("plain", [P, 64, T], F32)
        plain = guard.__enter__()
        guard.__exit__(None, None, None)
        parts = sb("parts", [P, 32, 2, T], F32R)
        raw = sb("raw", [P, RAW, 4, W])
        wsplit = sb("wsplit", [P, RING, 4, 2, W], F32R)
        xa = sb("xa", [P, NC, 2, T], F32R)
        x = sb("x", [P, NC, T])
        lohalf = sb("lohalf", [P, 2, 2, T])
        val = sb("val", [P, 2, T])
        t1 = sb("t1", [P, 2, T])
        work = sb("work", [P, 5, T])
        t2, gated = work[:, 0:2, :], work[:, 2:4, :]
        sq = sb("sq", [P, 2, 2, T])
        acc = sb("acc", [P, 2, T])
        root = sb("root", [P, T])
        rstd = sb("rstd", [P, T])
        rstd2 = sb("rstd2", [P, T])
        root_tok = sb("root_tok", [P, NT])
        rstd_tok = sb("rstd_tok", [P, NT])
        ident = sb("ident", [P, P])
        ones = sb("ones", [P, P])
        tri = sb("tri", [P, P])
        flip = sb("flip", [P, P])
        gain = sb("gain", [P, GAIN_N])
        taps = sb("taps", [P, NC, CONV_W])
        ropec = sb("ropec", [P, 1 + P])
        cos = sb("cos", [P, T])
        sin = sb("sin", [P, T])
        consts = sb("consts", [P, 2])
        blast = sb("blast", [P, 16])
        sbias = sb("sbias", [P, 2, ATT_G, T])
        logit = sb("logit", [P, 9 * P])
        probT = work[:, :, :].rearrange("p a b -> p (a b)")[:, 0:9 * P]
        wa2 = sbias[0:GLA_RANK + 1, 1, 0:2, :].rearrange("p a b -> p (a b)")
        ha = sbias[0:32, 1, 2, :]
        stat = sb("stat", [P, 8])
        gain_rows = logit[0:GAIN_N, 0:P]
        dw_rows = logit[0:CONV_W, P:P + D]
        relrow = t1[0:REL_BUCKETS + 1, 0, 0:ATT_G * ATT_H]
        onehot = probT[0:REL_BUCKETS + 1, :]
        posi = t1[:, 1, :].bitcast(I32)
        bias_dram = nc.dram_tensor("bias_rows", (ATT_G, ATT_H, BIAS_N), F32, kind="Internal").ap()

        ps = ctx.enter_context(nc.psum_tensor("ps", [P, 2, 2, 512], F32))
        misc = ctx.enter_context(nc.psum_tensor("misc", [P, 4, 512], F32))
        misc_flat = misc[:, :, :].rearrange("p a b -> p (a b)")

        def units(u, n=1):
            return plain[:, u:u + n, :]

        def flat(u, n=1):
            return plain[:, u:u + n, :].rearrange("p a b -> p (a b)")

        def bcast(ap, n):
            return ap.unsqueeze(1).to_broadcast([P, n, ap.shape[-1]])

        relout = flat(56, 5)[0:ATT_H, 0:ATT_G * BIAS_N]

        def rows(ap):
            return ap.rearrange("(k p) n -> p k n", p=P)

        def cols(ap, at=0, width=W):
            v = rows(ap)
            return lambda g, k, n: [(0, width, v[:, k:k + n, bass.ds(g * width + at, width)])]

        def pair_cols(a1, a2):
            v = rows(a1), rows(a2)
            return lambda g, k, n: [(0, W, v[g[1]][:, k:k + n, bass.ds(g[0] * W, W)])]

        def wide(ap, at, n):
            v = rows(ap)
            return lambda g, k, m: [(0, n, v[:, k:k + m, at:at + n])]

        def lora(ap, first, size, per_head, heads):
            v = ap.rearrange("(k p) h d -> p k h d", p=P)
            return lambda g, k, n: [(h * size, size, v[:, k:k + n, g * heads + h, first:first + size])
                                    for h in range(heads)]

        w_in = a["w_in"][0]
        K8 = [4, 4]
        K22 = [3, 3, 3, 3, 3, 3, 2, 2]
        K32 = [4] * 8

        def from_xa(k):
            return xa[:, k, :, :]

        def from_parts(c):
            return lambda k: parts[:, c + k, :, :]

        phases = []

        def add(*args, **kw):
            phases.append(Phase(*args, **kw))

        add("ha", wide(w_in, COL_HA, P), 1, K8, from_xa, ("ha",), width=P)
        add("gla_q", cols(w_in, 0), 2, K8, from_xa, ("keep", 0))
        add("gla_k", cols(w_in, GLA_QK), 2, K8, from_xa, ("keep", 4))
        add("gla_v", cols(w_in, 2 * GLA_QK), 4, K8, from_xa, ("keep_tok", 8), layout="T")
        add("hr", cols(w_in, 2 * GLA_QK + GLA_V), 4, K8, from_xa, ("func", ACT.Silu, 16))
        for g in range(ATT_G):
            at, u = COL_ATT + g * 3 * ATT_W, 24 + 12 * g
            add(f"att_q{g}", cols(w_in, at), 2, K8, from_xa, ("keep", u, float(HD) ** -0.5))
            add(f"att_k{g}", cols(w_in, at + ATT_W), 2, K8, from_xa, ("keep", u + 4))
            add(f"att_v{g}", cols(w_in, at + 2 * ATT_W), 2, K8, from_xa, ("keep_tok", u + 8), layout="T")
        add("gates", cols(w_in, COL_GATE), 8, K8, from_xa, ("func", ACT.Sigmoid, 0))
        add("y_gla", cols(a["w_o_gla"][0]), 4, K8, from_parts(12), ("times", 0))
        add("y_att", cols(a["w_o_attn"][0]), 4, [4], from_parts(20), ("mix", 0, 8, 24))
        add("w_out", cols(a["w_out"][0]), 4, K8, from_parts(24), ("resid", 1.0, GAIN_AT["ln2"]))
        add("mlp1", cols(a["w_mlp1"][0]), 16, K8, from_xa, ("relu2",), loop=(1, 4, 3))
        add("mlp2", cols(a["w_mlp2"][0]), 4, K32, from_parts(0), ("resid", 1.0, GAIN_AT["ln3"]))
        add("w_pg", cols(a["w_pg"][0]), 4, K8, from_xa, ("func", ACT.Sigmoid, 0))
        add("w_pp", cols(a["w_pp"][0]), 4, [2], from_parts(16), ("ple", 0))

        def ffn(w, i, nxt):
            add(f"{w}_up{i}", pair_cols(a[f"{w}_w1_2"][i], a[f"{w}_w3_2"][i]), 2 * FF2 // W, K8, from_xa,
                ("swiglu",), loop=(2, 4, 4))
            add(f"{w}_down{i}", cols(a[f"{w}_w2_2"][i]), 4, K22, from_parts(0), ("resid", 0.5, nxt))

        gn = GAIN_AT
        ffn("ffn1", 0, gn["mix_norm_2"])
        pw1 = a["conv_w_pw1_2"][0]
        add("pw1", pair_cols(pw1[:, D:2 * D], pw1[:, 0:D]), 8, K8, from_xa, ("glu",))
        add("pw2", cols(a["conv_w_pw2_2"][0]), 4, K8, from_parts(16), ("resid", 1.0, gn["ffn_norm2_2"]))
        ffn("ffn2", 0, gn["ffn_norm1_2"] + 8)
        ffn("ffn1", 1, gn["mix_norm_2"] + 8)
        w_a = a["mla_w_a_2"][0]
        add("mla_a", cols(w_a), 3, K8, from_xa, ("keep_sq", 0))
        krows = rows(w_a)[:, :, Q_LORA + KV_LORA:]
        add("mla_kr", lambda g, k, n: [(h * ROPE, ROPE, krows[:, k:k + n, :]) for h in range(2)],
            1, K8, from_xa, ("keep", 6), width=P)
        mla_scale = float(NOPE + ROPE) ** -0.5
        uq, ukv = a["mla_w_uq_2"][0], a["mla_w_ukv_2"][0]
        add("uq_nope", lora(uq, 0, NOPE, NOPE + ROPE, 2), 4, [4], from_parts(4), ("keep", 20, mla_scale))
        add("uq_rope", lora(uq, NOPE, ROPE, NOPE + ROPE, 4), 2, [4], from_parts(4), ("keep", 28, mla_scale))
        add("ukv_nope", lora(ukv, 0, NOPE, NOPE + VH, 2), 4, [2], from_parts(8), ("keep", 32))
        add("ukv_v", lora(ukv, NOPE, VH, NOPE + VH, 2), 4, [2], from_parts(8), ("keep_tok", 40), layout="T")
        add("w_o", cols(a["mla_w_o_2"][0]), 4, K8, from_parts(0), ("resid", 1.0, gn["ffn_norm2_2"] + 8))
        ffn("ffn2", 1, None)

        by = {p.name: p for p in phases}
        blocks, nblk, ngrp, ngate, nkept = [], 0, 0, 0, 0
        GATES = {"func": 1, "swiglu": 0.5, "glu": 0.5}
        for p in phases:
            p.block0, p.group0, p.gate0, p.kept0 = nblk, ngrp, ngate, nkept
            nkept += p.groups if p.evac[0] in ("ha", "keep", "keep_tok") else 0
            nblk += p.groups * len(p.kns)
            ngrp += p.groups
            ngate += int(p.groups * GATES.get(p.evac[0], 0))
            blocks += [(p, g, j) for g in range(p.groups) for j in range(len(p.kns))]
        moving, made = {}, 0
        for name, n in (("w_in", 8), ("ogla", 8), ("oatt", 4), ("mix", 8), ("mlp1", 8), ("mlp2", 32), ("w_pg", 8),
                        ("ple", 2), ("ffn1_up0", 8), ("ffn1_down0", 22), ("pw1", 8), ("conv", 8), ("ffn2_up0", 8),
                        ("ffn2_down0", 22), ("ffn1_up1", 8), ("ffn1_down1", 22), ("mla_a", 8), ("cq", 4),
                        ("ckv", 2), ("omla", 8), ("ffn2_up1", 8), ("ffn2_down1", 22)):
            moving[name] = made
            made += n
        source = {"y_gla": "ogla", "y_att": "oatt", "w_out": "mix", "w_pp": "ple", "pw2": "conv", "mla_kr": "mla_a",
                  "uq_nope": "cq", "uq_rope": "cq", "ukv_nope": "ckv", "ukv_v": "ckv", "w_o": "omla"}
        for p in phases:
            p.ready = moving[source.get(p.name, p.name if p.name in moving else "w_in")]
        after = {"w_out": "mlp1", "mlp2": "w_pg", "pw2": "ffn2_up0", "ffn1_down0": "pw1", "ffn2_down0": "ffn1_up1",
                 "ffn1_down1": "mla_a", "w_o": "ffn2_up1"}
        norms, pairs, sums = {}, {}, 0
        for name, n in (("w_in", 4), ("mlp1", 4), ("w_pg", 4), ("ln_f", 4), ("ffn1_up0", 4), ("pw1", 4), ("conv", 4),
                        ("ffn2_up0", 4), ("ffn1_up1", 4), ("mla_a", 4), ("cq", 2), ("ckv", 1), ("ffn2_up1", 4),
                        ("final", 4)):
            norms[name] = len(norms)
            pairs[name] = (sums, n)
            sums += n
        pair_of = {"w_out": "mlp1", "mlp2": "w_pg", "w_pp": "ln_f", "ffn1_down0": "pw1", "pw2": "ffn2_up0",
                   "ffn2_down0": "ffn1_up1", "ffn1_down1": "mla_a", "w_o": "ffn2_up1", "ffn2_down1": "final"}
        norm_at = {"gla_q": "w_in", "mlp1": "mlp1", "w_pg": "w_pg", "ffn1_up0": "ffn1_up0", "pw1": "pw1",
                   "ffn2_up0": "ffn2_up0", "ffn1_up1": "ffn1_up1", "mla_a": "mla_a", "ffn2_up1": "ffn2_up1",
                   "ha": "w_in"}
        del norm_at["gla_q"]

        s_rows = sem("s_rows")
        s_setup = sem("s_setup")
        s_x = sem("s_x")
        s_p = sem("s_p")
        s_rel = sem("s_rel")
        s_bias = [sem(f"s_bias{b}") for b in range(2)]
        s_out = sem("s_out")
        raw_landed = [sem(f"raw_landed{i}") for i in range(RAW)]
        hi_done = sem("hi_done")
        lo_done = sem("lo_done")
        used = sem("used")
        lohalf_done = sem("lohalf_done")
        val_done = sem("val_done")
        ready = sem("ready")
        gate_in = sem("gate_in")
        gate_out = sem("gate_out")
        new_x = sem("new_x")
        squared = sem("squared")
        summed = sem("summed")
        norm_sum = sem("norm_sum")
        norm_root = sem("norm_root")
        norm_read = sem("norm_read")
        kept = sem("kept")
        const_ready = sem("const_ready")
        dve = sem("dve")
        actq = sem("actq")
        pool = sem("pool")
        s_pe = sem("s_pe")
        s_dv = sem("s_dv")
        s_ac = sem("s_ac")

        order = {"pe": {}, "dv": {}, "ac": {}}

        def name_steps(engine, names):
            for n in names:
                order[engine][n] = len(order[engine]) + 1

        heads = [f"att{h}" for h in range(ATT_H)]
        mheads = [f"mla{h}" for h in range(MLA_H)]
        name_steps("pe", ["gainT", "tapsT", "rel"] + [f"xT{c}" for c in range(4)]
                   + ["z", "cum", "scores", "koutT", "upd0", "upd1", "upd2", "o", "osum"]
                   + [f"{h}.{s}" for h in heads for s in ("qk", "pT", "pv")]
                   + ["pT"] + ["rope_q0", "rope_q1", "rope_k"]
                   + [f"{h}.{s}" for h in mheads for s in ("qk", "pT", "pv")] + ["outT"])
        name_steps("dv", ["gain", "taps", "rel", "trig", "setup", "z", "abs", "log", "b", "blast", "gla_in", "attn"]
                   + ["st0", "st1", "st2", "osq", "og"]
                   + [f"{h}.{s}" for h in heads for s in ("max", "norm", "o")]
                   + ["ple_free", "lnf", "conv", "convn", "cqn", "ckvn", "rope_q", "rope_k"]
                   + [f"{h}.{s}" for h in mheads for s in ("max", "norm", "o")] + ["final", "out"])
        name_steps("ac", ["trig", "log", "expb", "expd", "ktok", "o", "oroot"]
                   + [f"{h}.{s}" for h in heads for s in ("exp", "pT")]
                   + ["conv"] + [f"{h}.{s}" for h in mheads for s in ("exp", "pT")])

        def pe_did(e, n):
            e.wait_ge(s_pe, order["pe"][n])

        def dv_did(e, n):
            e.wait_ge(s_dv, order["dv"][n])

        def ac_did(e, n):
            e.wait_ge(s_ac, order["ac"][n])

        def locate(s):
            return blocks[s]

        block = ctx.enter_context(nc.Block())

        @block.sync
        def _(sp):
            at = 0
            for name, n in GAINS:
                v = a[name]
                v = v if len(v.shape) == 1 else v.rearrange("a n -> (a n)")
                sp.dma_start(gain_rows[at:at + n, :], v.rearrange("(c p) -> c p", p=P)).then_inc(s_rows, 16)
                at += n
            sp.dma_start(dw_rows, a["conv_w_dw_2"][0]).then_inc(s_rows, 16)
            sp.dma_start(flat(0, 8).rearrange("p (t n) -> p t n", t=NT),
                         a["x"][0].rearrange("(t p) n -> p t n", p=P)).then_inc(s_x, 16)
            sp.dma_start(ropec[:, :], a["rope_c"]).then_inc(s_setup, 16)
            sp.dma_start(posi, a["positions_2"][0].partition_broadcast(P)).then_inc(s_setup, 16)
            sp.dma_start(onehot, a["bias_c"].rearrange("b g j -> b (g j)")).then_inc(s_setup, 16)
            sp.dma_start(relrow[0:REL_BUCKETS, :], a["rel_bias"]).then_inc(s_setup, 16)
            sp.dma_start(wa2[0:GLA_RANK, :], a["w_a2"][0]).then_inc(s_setup, 16)
            sp.dma_start(wa2[GLA_RANK:GLA_RANK + 1, :], a["b_a"]).then_inc(s_setup, 16)

            def load(p, g, j, s0, i, per):
                if s0 >= RAW:
                    sp.wait_ge(lo_done, lin(s0 - RAW + 1, RING, i))
                kn = p.kns[j]
                if p.evac[0] in ("swiglu", "glu"):
                    where = (lin(g // 2, per // 2, i), g % 2)
                else:
                    where = lin(g, per, i)
                pieces = p.src(where, p.k0[j], kn)
                for c, n, src in pieces:
                    sp.dma_start(raw[:, s0 % RAW, 0:kn, c:c + n], src).then_inc(raw_landed[s0 % RAW], 16)

            for p in phases:
                for groups, turns in p.segments():
                    if turns is None:
                        for g in groups:
                            for j in range(len(p.kns)):
                                load(p, g, j, p.block(g, j), None, 0)
                    else:
                        with sp.Fori(0, turns) as i:
                            for g in groups:
                                for j in range(len(p.kns)):
                                    load(p, g, j, p.block(g, j), i, len(groups))
            dv_did(sp, "out")
            sp.dma_start(out[0].rearrange("(t p) n -> p t n", p=P),
                         flat(0, 8).rearrange("p (t n) -> p t n", t=NT)).then_inc(s_out, 16)
            sp.wait_ge(s_out, 16)

        landed, tally = [], [0] * RAW
        for s, (p, g, j) in enumerate(blocks):
            tally[s % RAW] += 16 * len(p.src((0, 0) if p.evac[0] in ("swiglu", "glu") else 0, 0, 1))
            landed.append(tally[s % RAW])

        @block.tensor
        def _(pe):
            mm = nc.tensor.matmul

            def product_group(p, g, i, per, first):
                bank = (p.group0 + g) % 2
                if p.group0 + g >= 2:
                    pe.wait_ge(val_done, lin(p.group0 + g - 1, per, i))
                nk = sum(p.kns)
                for j, kn in enumerate(p.kns):
                    s = p.block(g, j)
                    slot = s % RING
                    pe.wait_ge(lo_done, lin(s + 1, RING if i is not None else 0, i))
                    for kk in range(kn):
                        k = p.k0[j] + kk
                        if first:
                            pe.wait_ge(ready, p.ready + k + 1)
                        mov = p.moving(k)
                        wboth = wsplit[:, slot, kk, :, :]
                        for c in range(p.width // P):
                            o = ps[:, bank, c, :]
                            st, en = k == 0, k == nk - 1
                            if p.layout == "F":
                                mm(o, wboth[:, 0, c * P:(c + 1) * P], mov.rearrange("p h t -> p (h t)"),
                                   start=st, stop=False, skip_group_check=True)
                                last = mm(o[:, T:2 * T], wboth[:, 1, c * P:(c + 1) * P], mov[:, 0, :],
                                          start=False, stop=en, skip_group_check=True)
                            else:
                                mm(o, mov[:, 0, c * P:(c + 1) * P], wboth.rearrange("p h n -> p (h n)"),
                                   start=st, stop=False, skip_group_check=True)
                                last = mm(o[:, T:2 * T], mov[:, 1, c * P:(c + 1) * P], wboth[:, 0, :],
                                          start=False, stop=en, skip_group_check=True)
                    last.then_inc(used, 1)

            def norm_sum_step(name, width=2, token=False):
                q, n = pairs[name]
                pe.wait_ge(summed, q + n)
                if norms[name] >= 1:
                    pe.wait_ge(norm_root, norms[name])
                for c in range(2):
                    last = mm(misc[:, 3, 0:T], ones[:, :], acc[:, c, :], start=(c == 0), stop=(c == 1),
                              skip_group_check=True)
                if token:
                    for t in range(NT):
                        for c in range(2):
                            last = mm(misc[:, 3, T + t:T + t + 1], acc[:, c, t * P:(t + 1) * P], ones[:, 0:1],
                                      start=False, stop=(c == 1), skip_group_check=True)
                last.then_inc(norm_sum, 1)

            def transpose_to(dst, src, n=P):
                return nc.tensor.transpose(dst, src, ident[0:n, 0:n])

            pe.wait_ge(const_ready, 1)
            pe.wait_ge(s_rows, 16 * (len(GAINS) + 1))
            transpose_to(ps[:, 0, 0, 0:GAIN_N], gain_rows, GAIN_N).then_inc(s_pe, 1)
            for c in range(NC):
                last = transpose_to(ps[:, 0, 1, c * 32:c * 32 + CONV_W], dw_rows[:, c * P:(c + 1) * P], CONV_W)
            last.then_inc(s_pe, 1)
            pe.wait_ge(s_setup, 16 * 6)
            for g in range(ATT_G):
                last = mm(ps[0:ATT_H, 1, g % 2, 0:BIAS_N] if g < 2 else misc[0:ATT_H, 3, 0:BIAS_N],
                          relrow[:, g * ATT_H:(g + 1) * ATT_H], onehot[:, g * BIAS_N:(g + 1) * BIAS_N],
                          start=True, stop=True)
            last.then_inc(s_pe, 1)
            pe.wait_ge(s_x, 16)
            xrow = flat(0, 8).rearrange("p (t n) -> p t n", t=NT)
            for q in range(4):
                if q == 3:
                    dv_did(pe, "rel")
                for c in range(2):
                    for t in range(NT):
                        k = 2 * q + c
                        last = transpose_to(misc[:, q, c * T + t * P:c * T + (t + 1) * P],
                                            xrow[:, t, k * P:(k + 1) * P])
                last.then_inc(s_pe, 1)

            def gla_step(k):
                if k == 0:
                    pe.wait_ge(kept, 1)
                    for t in range(NT):
                        last = mm(misc[:, t, :], ha[0:GLA_RANK + 1, t * P:(t + 1) * P], wa2,
                                  start=True, stop=True)
                    last.then_inc(s_pe, 1)
                if k == 1:
                    dv_did(pe, "log")
                    for h in range(GLA_H):
                        for t in range(NT):
                            last = mm(misc_flat[:, h * T + t * P:h * T + (t + 1) * P],
                                      flat(32, 4)[:, t * GLA_QK + h * P:t * GLA_QK + (h + 1) * P], tri[:, :],
                                      start=True, stop=True, skip_group_check=True)
                    last.then_inc(s_pe, 1)
                if k == 2:
                    dv_did(pe, "gla_in")
                    for h in range(GLA_H):
                        for t in range(NT):
                            last = mm(misc_flat[:, (h * NT + t) * P:(h * NT + t + 1) * P],
                                      plain[:, 28 + h, t * P:(t + 1) * P], plain[:, h, t * P:(t + 1) * P],
                                      start=True, stop=True, skip_group_check=True)
                    last.then_inc(s_pe, 1)
                    for h in range(GLA_H):
                        for t in range(NT):
                            last = transpose_to(misc_flat[:, 1024 + (h * NT + t) * P:1024 + (h * NT + t + 1) * P],
                                                plain[:, 4 + h, t * P:(t + 1) * P])
                    last.then_inc(s_pe, 1)
                if k == 3:
                    ac_did(pe, "ktok")
                    dv_did(pe, "attn")
                    for n in range(3):
                        if n == 2:
                            dv_did(pe, "st0")
                        t, r = n // 2, (n % 2) * GLA_CHUNK
                        for h in range(GLA_H):
                            at = (n % 2) * 1024 + h * GLA_DV
                            last = mm(misc_flat[:, at:at + GLA_DV],
                                      flat(40, 4)[r:r + GLA_CHUNK, (h * NT + t) * P:(h * NT + t + 1) * P],
                                      plain[r:r + GLA_CHUNK, 8 + 2 * h + t, :],
                                      start=True, stop=True, skip_group_check=True)
                        last.then_inc(s_pe, 1)
                if k == 4:
                    dv_did(pe, "st2")
                    for h in range(GLA_H):
                        for vh in range(2):
                            c = 2 * h + vh
                            o = misc_flat[:, c * T:(c + 1) * T]
                            for t in range(NT):
                                mm(o[:, t * P:(t + 1) * P], plain[:, 8 + 2 * h + t, vh * P:(vh + 1) * P],
                                   flat(44, 4)[:, (h * NT + t) * P:(h * NT + t + 1) * P],
                                   start=(t == 0), stop=False, skip_group_check=True)
                            for n in range(1, 4):
                                last = mm(o[:, n * GLA_CHUNK:(n + 1) * GLA_CHUNK],
                                          plain[:, 52 + (n - 1) * GLA_H + h, vh * P:(vh + 1) * P],
                                          plain[:, h, n * GLA_CHUNK:(n + 1) * GLA_CHUNK],
                                          start=False, stop=(n == 3), skip_group_check=True)
                    last.then_inc(s_pe, 1)
                if k == 5:
                    dv_did(pe, "osq")
                    for h in range(GLA_H):
                        for vh in range(2):
                            last = mm(misc_flat[:, h * T:(h + 1) * T], ones[:, :], plain[:, 32 + 2 * h + vh, :],
                                      start=(vh == 0), stop=(vh == 1), skip_group_check=True)
                    last.then_inc(s_pe, 1)

            def attend(name, step, ng, qk, value, bias):
                if step == "qk":
                    for g in range(ng):
                        for t, o in ((0, misc[:, 0, g * P:(g + 1) * P]),
                                     (1, misc[:, 1 + g // 2, (g % 2) * T:(g % 2) * T + T])):
                            terms = qk(g)
                            for n, (q, k) in enumerate(terms):
                                mm(o, q[:, t * P:(t + 1) * P], k[:, 0:(t + 1) * P], start=(n == 0), stop=False,
                                   skip_group_check=True)
                            last = mm(o, flip[:, :], bias[:, g, (1 - t) * P:T], start=False, stop=True,
                                      skip_group_check=True)
                    last.then_inc(s_pe, 1)
                if step == "pT":
                    dv_did(pe, f"{name}.norm")
                    for n in range(3 * ng):
                        o = misc[:, 0, n * P:(n + 1) * P] if n < ng else misc_flat[:, 512 + (n - ng) * P:
                                                                                   512 + (n - ng + 1) * P]
                        last = transpose_to(o, logit[:, n * P:(n + 1) * P])
                    last.then_inc(s_pe, 1)
                if step == "pv":
                    ac_did(pe, f"{name}.pT")
                    o = misc[:, 3, 0:T]
                    for g in range(ng):
                        mm(o[:, 0:P], value(g, 0), probT[:, g * P:(g + 1) * P], start=(g == 0), stop=False,
                           skip_group_check=True)
                    for g in range(ng):
                        for t in range(NT):
                            n = ng + 2 * g + t
                            last = mm(o[:, P:T], value(g, t), probT[:, n * P:(n + 1) * P],
                                      start=False, stop=(g == ng - 1 and t == 1), skip_group_check=True)
                    last.then_inc(s_pe, 1)

            def att_head(h, step):
                if step == "qk":
                    pe.wait_ge(s_bias[h % 2], 16 * (h // 2 + 1))
                    if h == 0:
                        pe.wait_ge(kept, by["att_v2"].kept0 + 2)
                        dv_did(pe, "og")
                    else:
                        dv_did(pe, f"att{h - 1}.o")
                attend(f"att{h}", step, ATT_G, lambda g: [(plain[:, 24 + 12 * g + h, :], plain[:, 28 + 12 * g + h, :])],
                       lambda g, t: plain[:, 32 + 12 * g + 2 * (h // 2) + t, (h % 2) * P:(h % 2) * P + P],
                       sbias[:, h % 2, :, :])

            def mla_head(h, step):
                if step == "qk":
                    if h == 0:
                        dv_did(pe, "rope_k")
                    else:
                        dv_did(pe, f"mla{h - 1}.o")
                r = (h % 2) * ROPE
                attend(f"mla{h}", step, 1,
                       lambda g: [(plain[:, 20 + h, :], plain[:, 32 + h, :]),
                                  (plain[r:r + ROPE, 28 + h // 2, :], plain[r:r + ROPE, 6, :])],
                       lambda g, t: plain[:, 40 + 2 * (h // 2) + t, (h % 2) * P:(h % 2) * P + P],
                       sbias[:, 0, 0:1, :])

            for p in phases:
                for groups, turns in p.segments():
                    if turns is not None:
                        with pe.Fori(0, turns) as i:
                            for g in groups:
                                product_group(p, g, i, len(groups), False)
                        continue
                    for g in groups:
                        product_group(p, g, None, 0, g == 0)
                        if g == 0 and p.name in norm_at:
                            norm_sum_step(norm_at[p.name], token=p.name == "ha")
                        if p.name == "hr":
                            gla_step(g)
                        if p.name == "gates" and g % 2 == 0:
                            att_head(g // 2, "qk")
                        if p.name == "gates" and g % 2 == 1:
                            att_head(g // 2, "pT")
                            att_head(g // 2, "pv")
                        if p.name == "w_pg" and g == 2:
                            pe.wait_ge(s_p, 16)
                            for k in range(2):
                                for t in range(NT):
                                    last = transpose_to(misc[:, 0, k * T + t * P:k * T + (t + 1) * P],
                                                        plain[:, 40 + t, k * P:(k + 1) * P])
                            last.then_inc(s_pe, 1)
                if p.name == "hr":
                    gla_step(4)
                    gla_step(5)
                if p.name == "w_pp":
                    norm_sum_step("ln_f")
                if p.name == "pw1":
                    norm_sum_step("conv")
                if p.name == "mla_kr":
                    norm_sum_step("cq")
                    norm_sum_step("ckv", token=True)
                if p.name == "ukv_v":
                    pe.wait_ge(kept, by["ukv_v"].kept0 + 4)
                    for n in range(2):
                        for c in range(2):
                            last = mm(misc[:, n, c * T:(c + 1) * T], ropec[:, 1:1 + P], plain[:, 28 + 2 * n + c, :],
                                      start=(c == 0), stop=(c == 1), skip_group_check=True)
                        last.then_inc(s_pe, 1)
                    mm(misc[:, 2, 0:T], ropec[:, 1:1 + P], plain[:, 6, :], start=True, stop=True).then_inc(s_pe, 1)
                    for h in range(MLA_H):
                        for step in ("qk", "pT", "pv"):
                            mla_head(h, step)
            norm_sum_step("final")
            dv_did(pe, "final")
            for k in range(NC):
                for t in range(NT):
                    n = k * NT + t
                    last = transpose_to(misc_flat[:, t * D + k * P:t * D + (k + 1) * P],
                                        plain[:, 8 + k, t * P:(t + 1) * P])
            last.then_inc(s_pe, 1)

        @block.scalar
        def _(act):
            act_fn = nc.scalar.activation
            mine = [0]

            def step(ins):
                mine[0] += 1
                ins.then_inc(actq, 1)
                act.wait_ge(actq, mine[0])

            sides = [0]

            def settle():
                sides[0] += 1
                act.wait_ge(s_ac, sides[0])

            def round_block(p, g, j, s0, i):
                slot, kn = s0 % RING, p.kns[j]
                act.wait_ge(raw_landed[s0 % RAW], lin(landed[s0], 16 * RING // RAW, i))
                if s0 >= RING:
                    act.wait_ge(used, lin(s0 - RING + 1, RING, i))
                nc.scalar.copy(wsplit[:, slot, 0:kn, 0, 0:p.width], raw[:, s0 % RAW, 0:kn, 0:p.width]
                               ).then_inc(hi_done, 1)

            def ahead(p, g, j, i):
                s = p.block(g, j) + AHEAD
                if i is None:
                    if s < len(blocks):
                        round_block(*locate(s), s, None)
                else:
                    o = g * len(p.kns) + j + AHEAD
                    round_block(p, o // len(p.kns), o % len(p.kns), s, i)

            def take_lohalf(p, g, i, per):
                G = p.group0 + g
                nch = p.width // P
                act.wait_ge(used, lin(p.block(g, len(p.kns) - 1) + 1, RING if i is not None else 0, i))
                if G >= 2:
                    act.wait_ge(val_done, lin(G - 1, per, i))
                nc.scalar.copy(lohalf[:, G % 2, 0:nch, :], ps[:, G % 2, 0:nch, T:2 * T]).then_inc(lohalf_done, 1)

            def square_pair(name, c, src):
                q = pairs[name][0] + c
                act.wait_ge(new_x, q + 1)
                if q >= 2:
                    act.wait_ge(summed, q - 1)
                act_fn(sq[:, q % 2, :, :], src, ACT.Square).then_inc(squared, 1)

            def norm_step(name, features=D, token=False):
                n = norms[name]
                act.wait_ge(norm_sum, n + 1)
                if n >= 1:
                    act.wait_ge(norm_read, n)
                last = act_fn(root[:, :], misc[:, 3, 0:T], ACT.Sqrt, bias=consts[:, 0:1], scale=1.0 / features)
                if token:
                    last = act_fn(root_tok[:, :], misc[:, 3, T:T + NT], ACT.Sqrt, bias=consts[:, 0:1],
                                  scale=1.0 / features)
                last.then_inc(norm_root, 1)

            def evacuate(p, g, i, per):
                kind = p.evac[0]
                take_lohalf(p, g, i, per)
                if kind == "func":
                    n = p.gate0 + g
                    act.wait_ge(gate_in, n + 1)
                    act_fn(units(p.evac[2] + 2 * g, 2), t1[:, :, :], p.evac[1]).then_inc(gate_out, 1)
                if kind in ("swiglu", "glu") and g % 2 == 0:
                    n = p.gate0 + g // 2
                    act.wait_ge(gate_in, lin(n + 1, per // 2, i))
                    act_fn(gated[:, :, :], t1[:, :, :], ACT.Silu if kind == "swiglu" else ACT.Sigmoid
                           ).then_inc(gate_out, 1)
                if kind in ("resid", "ple"):
                    square_pair(pair_of[p.name], g, x[:, 2 * g:2 * g + 2, :])
                if kind == "keep_sq":
                    square_pair("cq" if g < 2 else "ckv", g % 2, units(2 * g, 2))

            def gla_step(k):
                if k == 0:
                    dv_did(act, "abs")
                    step(act_fn(flat(28, 4), flat(28, 4), ACT.Exp, scale=-1.0))
                    nc.scalar.activation(flat(28, 4), flat(28, 4), ACT.Ln, bias=1.0).then_inc(s_ac, 1)
                    settle()
                if k == 1:
                    dv_did(act, "b")
                    act_fn(flat(40, 4), flat(36, 4), ACT.Exp)
                    act_fn(flat(44, 4), flat(36, 4), ACT.Exp, scale=-1.0).then_inc(s_ac, 1)
                    settle()
                    dv_did(act, "blast")
                    act_fn(blast[:, :], blast[:, :], ACT.Exp)
                    act_fn(flat(48, 4), flat(48, 4), ACT.Exp).then_inc(s_ac, 1)
                    settle()
                if k == 2:
                    pe_did(act, "koutT")
                    dv_did(act, "gla_in")
                    nc.scalar.copy(flat(40, 4), misc_flat[:, 1024:2048]).then_inc(s_ac, 1)
                    settle()
                if k == 4:
                    pe_did(act, "o")
                    nc.scalar.copy(flat(24, 8), misc_flat[:, :]).then_inc(s_ac, 1)
                    settle()
                if k == 5:
                    pe_did(act, "osum")
                    act_fn(flat(48, 4), misc_flat[:, 0:1024], ACT.Sqrt, bias=consts[:, 0:1], scale=1.0 / GLA_DV
                           ).then_inc(s_ac, 1)
                    settle()

            def attend(name, ng):
                n0 = ng * P
                dv_did(act, f"{name}.max")
                act_fn(logit[:, 0:n0], misc[:, 0, 0:n0], ACT.Exp, bias=stat[:, 2:3], accum_out=stat[:, 4:5])
                act_fn(logit[:, n0:3 * n0], misc_flat[:, 512:512 + 2 * n0], ACT.Exp, bias=stat[:, 3:4],
                       accum_out=stat[:, 5:6]).then_inc(s_ac, 1)
                settle()
                pe_did(act, f"{name}.pT")
                nc.scalar.copy(probT[:, 0:n0], misc[:, 0, 0:n0])
                nc.scalar.copy(probT[:, n0:3 * n0], misc_flat[:, 512:512 + 2 * n0]).then_inc(s_ac, 1)
                settle()

            for s in range(AHEAD):
                round_block(*locate(s), s, None)
            act.wait_ge(const_ready, 1)
            for c in range(4):
                square_pair("w_in", c, x[:, 2 * c:2 * c + 2, :])
            dv_did(act, "trig")
            act_fn(sin[:, :], root[:, :], ACT.Sin, scale=0.5)
            act_fn(cos[:, :], rstd[:, :], ACT.Sin, scale=-0.5, bias=consts[:, 1:2]).then_inc(s_ac, 1)
            settle()

            for p in phases:
                for groups, turns in p.segments():
                    if turns is not None:
                        with act.Fori(0, turns) as i:
                            for g in groups:
                                for j in range(len(p.kns)):
                                    ahead(p, g, j, i)
                                evacuate(p, g, i, len(groups))
                        continue
                    for g in groups:
                        for j in range(len(p.kns)):
                            ahead(p, g, j, None)
                        if g == 0 and p.name in norm_at:
                            norm_step(norm_at[p.name], token=p.name == "ha")
                        evacuate(p, g, None, 0)
                        if p.name == "hr":
                            gla_step(g)
                        if p.name == "gates" and g % 2 == 1:
                            attend(f"att{g // 2}", ATT_G)
                if p.name == "hr":
                    gla_step(4)
                    gla_step(5)
                if p.name == "w_pp":
                    norm_step("ln_f")
                    for c in range(4):
                        square_pair("ffn1_up0", c, x[:, 2 * c:2 * c + 2, :])
                if p.name == "pw1":
                    for c in range(4):
                        square_pair("conv", c, units(10 + 2 * c, 2))
                    norm_step("conv")
                    dv_did(act, "convn")
                    act_fn(units(10, 8), units(10, 8), ACT.Silu).then_inc(s_ac, 1)
                    settle()
                if p.name == "mla_kr":
                    norm_step("cq", Q_LORA)
                    norm_step("ckv", KV_LORA, token=True)
                if p.name == "ukv_v":
                    for h in range(MLA_H):
                        attend(f"mla{h}", 1)
            norm_step("final")

        @block.vector
        def _(v):
            vec = nc.vector
            TT, TS, STT = vec.tensor_tensor, vec.tensor_scalar, vec.scalar_tensor_tensor
            mine = [0]
            loop = [None, 0]

            def step(ins):
                mine[0] += 1
                ins.then_inc(dve, 1)
                v.wait_ge(dve, lin(mine[0], loop[1], loop[0]))

            def done(name, ins):
                ins.then_inc(s_dv, 1)
                v.wait_ge(s_dv, order["dv"][name])

            def keep(p, g, ins):
                ins.then_inc(kept, 1)
                v.wait_ge(kept, p.kept0 + g + 1)

            def rest_block(p, g, j, s0, i):
                slot, kn = s0 % RING, p.kns[j]
                v.wait_ge(hi_done, lin(s0 + 1, RING, i))
                TT(wsplit[:, slot, 0:kn, 1, 0:p.width], raw[:, s0 % RAW, 0:kn, 0:p.width],
                   wsplit[:, slot, 0:kn, 0, 0:p.width].bitcast(F32), ALU.subtract).then_inc(lo_done, 1)

            def ahead(p, g, j, i):
                s = p.block(g, j) + AHEAD
                if i is None:
                    if s < len(blocks):
                        rest_block(*locate(s), s, None)
                else:
                    o = g * len(p.kns) + j + AHEAD
                    rest_block(p, o // len(p.kns), o % len(p.kns), s, i)

            def split_gained(dst, src, at, n):
                for c in range(n):
                    ins = TS(dst[:, c, 0, :], src[:, c, :], gain[:, at + c:at + c + 1], None, ALU.mult)
                step(ins)
                for c in range(n):
                    STT(dst[:, c, 1, :], src[:, c, :], gain[:, at + c:at + c + 1], dst[:, c, 0, :].bitcast(F32),
                        ALU.mult, ALU.subtract).then_inc(ready, 1)

            def split(dst, src, n):
                step(vec.tensor_copy(dst[:, :, 0, :], src))
                TT(dst[:, :, 1, :], src, dst[:, :, 0, :].bitcast(F32), ALU.subtract).then_inc(ready, n)

            def norm_step(name, dst=rstd, token=False):
                v.wait_ge(norm_root, norms[name] + 1)
                if token:
                    step(vec.reciprocal(rstd_tok[:, :], root_tok[:, :]))
                vec.reciprocal(dst[:, :], root[:, :]).then_inc(norm_read, 1)
                v.wait_ge(norm_read, norms[name] + 1)

            def total(p, g, i, per, nparts=P):
                G, nch = p.group0 + g, p.width // P
                v.wait_ge(lohalf_done, lin(G + 1, per, i))
                TT(val[0:nparts, 0:nch, :], ps[0:nparts, G % 2, 0:nch, 0:T], lohalf[0:nparts, G % 2, 0:nch, :],
                   ALU.add).then_inc(val_done, 1)
                v.wait_ge(val_done, lin(G + 1, per, i))

            def evacuate(p, g, i, per):
                kind, nch = p.evac[0], p.width // P
                r2 = bcast(rstd[:, :], nch)
                total(p, g, i, per, GLA_RANK if kind == "ha" else P)
                if kind == "ha":
                    keep(p, g, TT(ha[0:GLA_RANK, :], val[0:GLA_RANK, 0, :], rstd[0:GLA_RANK, :], ALU.mult))
                if kind == "keep":
                    r = rstd2 if p.name in ("ukv_nope",) else rstd
                    scale = p.evac[2] if len(p.evac) > 2 else 1.0
                    keep(p, g, STT(units(p.evac[1] + 2 * g, nch), val[:, 0:nch, :], scale, bcast(r[:, :], nch),
                                   ALU.mult, ALU.mult))
                if kind == "keep_sq":
                    name, c = ("cq" if g < 2 else "ckv"), g % 2
                    TT(units(2 * g, 2), val[:, :, :], r2, ALU.mult).then_inc(new_x, 1)
                    v.wait_ge(new_x, pairs[name][0] + c + 1)
                if kind == "keep_tok":
                    for t in range(NT):
                        ins = TS(plain[:, p.evac[1] + 2 * g + t, :], val[:, t, :], rstd_tok[:, t:t + 1], None, ALU.mult)
                    keep(p, g, ins)
                if kind == "func":
                    n = p.gate0 + g
                    if n >= 1:
                        v.wait_ge(gate_out, n)
                    TT(t1[:, :, :], val[:, :, :], r2, ALU.mult).then_inc(gate_in, 1)
                    v.wait_ge(gate_in, n + 1)
                if kind in ("swiglu", "glu") and g % 2 == 0:
                    n = p.gate0 + g // 2
                    v.wait_ge(gate_out, lin(n, per // 2, i))
                    TT(t1[:, :, :], val[:, :, :], r2, ALU.mult).then_inc(gate_in, 1)
                    v.wait_ge(gate_in, lin(n + 1, per // 2, i))
                if kind in ("swiglu", "glu") and g % 2 == 1:
                    n, c = p.gate0 + g // 2, lin(g - 1, per, i)
                    step(TT(t2[:, :, :], val[:, :, :], r2, ALU.mult))
                    v.wait_ge(gate_out, lin(n + 1, per // 2, i))
                    if kind == "glu":
                        step(TT(upad[:, g - 1:g + 1, CONV_W - 1:], t2[:, :, :], gated[:, :, :], ALU.mult))
                    else:
                        step(TT(t2[:, :, :], t2[:, :, :], gated[:, :, :], ALU.mult))
                        split(parts[:, bass.ds(c, 2), :, :], t2[:, :, :], 2)
                if kind == "relu2":
                    c = lin(2 * g, 2 * per, i)
                    step(STT(t1[:, :, :], val[:, :, :], 0.0, r2, ALU.max, ALU.mult))
                    step(TT(t2[:, :, :], t1[:, :, :], t1[:, :, :], ALU.mult))
                    split(parts[:, bass.ds(c, 2), :, :], t2[:, :, :], 2)
                if kind == "times":
                    v.wait_ge(gate_out, by["gates"].gate0 + 8)
                    u = p.evac[1] + 2 * g
                    step(TT(units(u, 2), val[:, :, :], units(u, 2), ALU.mult))
                if kind == "mix":
                    u, w = p.evac[1] + 2 * g, p.evac[2] + 2 * g
                    step(TT(t2[:, :, :], val[:, :, :], units(w, 2), ALU.mult))
                    step(TT(t2[:, :, :], t2[:, :, :], units(u, 2), ALU.add))
                    split(parts[:, p.evac[3] + 2 * g:p.evac[3] + 2 * g + 2, :, :], t2[:, :, :], 2)
                if kind == "resid":
                    xs = x[:, 2 * g:2 * g + 2, :]
                    STT(xs, val[:, :, :], p.evac[1], xs, ALU.mult, ALU.add).then_inc(new_x, 1)
                    v.wait_ge(new_x, pairs[pair_of[p.name]][0] + g + 1)
                    if p.evac[2] is not None:
                        split_gained(xa[:, 2 * g:2 * g + 2, :, :], xs, p.evac[2] + 2 * g, 2)
                if kind == "ple":
                    v.wait_ge(gate_out, by["w_pg"].gate0 + 4)
                    xs = x[:, 2 * g:2 * g + 2, :]
                    step(TT(t2[:, :, :], val[:, :, :], units(2 * g, 2), ALU.mult))
                    TT(xs, xs, t2[:, :, :], ALU.add).then_inc(new_x, 1)
                    v.wait_ge(new_x, pairs[pair_of[p.name]][0] + g + 1)

            upad = flat(0, 9)[:, 0:NC * (T + CONV_W - 1)].rearrange("p (c t) -> p c t", c=NC)

            def gla_step(k):
                b3 = flat(36, 4).rearrange("p (h c t) -> p h c t", h=GLA_H, c=4)
                if k == 0:
                    pe_did(v, "z")
                    done("z", vec.tensor_copy(flat(24, 4), misc_flat[:, 0:1024]))
                    done("abs", STT(flat(28, 4), flat(24, 4), -1.0, flat(24, 4), ALU.mult, ALU.max))
                    ac_did(v, "log")
                    done("log", STT(flat(32, 4), flat(24, 4), 0.0, flat(28, 4), ALU.min, ALU.subtract))
                if k == 1:
                    pe_did(v, "cum")
                    done("b", vec.tensor_copy(flat(36, 4), misc_flat[:, 0:1024]))
                    bl = b3[:, :, :, GLA_CHUNK - 1:GLA_CHUNK].rearrange("p h c t -> p (h c t)")
                    step(vec.tensor_copy(blast[:, :], bl))
                    done("blast", TT(flat(48, 4).rearrange("p (n t) -> p n t", n=16),
                                     blast[:, :].unsqueeze(2).to_broadcast([P, 16, GLA_CHUNK]),
                                     flat(36, 4).rearrange("p (n t) -> p n t", n=16), ALU.subtract))
                    ac_did(v, "expd")
                    step(STT(flat(0, 4), flat(0, 4), float(GLA_DK) ** -0.5, flat(40, 4), ALU.mult, ALU.mult))
                    step(TT(flat(28, 4), flat(4, 4), flat(44, 4), ALU.mult))
                    done("gla_in", TT(flat(4, 4), flat(4, 4), flat(48, 4), ALU.mult))
                    step(vec.memset(flat(44, 4), 0.0))
                if k == 2:
                    pe_did(v, "scores")
                    done("attn", vec.copy_predicated(
                        flat(44, 4).rearrange("p (n t) -> p n t", n=8), bcast(tri[:, :].bitcast(I32), 8),
                        misc_flat[:, 0:1024].rearrange("p (n t) -> p n t", n=8)))
                if k == 3:
                    pe_did(v, "upd0")
                    v.wait_ge(s_rel, 16)
                    done("st0", vec.tensor_copy(flat(52, 4), misc_flat[:, 0:1024]))
                    for n in (1, 2):
                        pe_did(v, f"upd{n}")
                        for h in range(GLA_H):
                            at = (n % 2) * 1024 + h * GLA_DV
                            ins = STT(plain[:, 52 + n * 4 + h, :], plain[:, 48 + n * 4 + h, :],
                                      blast[:, h * 4 + n:h * 4 + n + 1], misc_flat[:, at:at + GLA_DV],
                                      ALU.mult, ALU.add)
                        done(f"st{n}", ins)
                if k == 4:
                    ac_did(v, "o")
                    done("osq", TT(flat(32, 8), flat(24, 8), flat(24, 8), ALU.mult))
                if k == 5:
                    v.wait_ge(gate_out, by["hr"].gate0 + 4)
                    ac_did(v, "oroot")
                    step(vec.reciprocal(flat(48, 4), flat(48, 4)))
                    rg = plain[:, 48:52, :].unsqueeze(2).to_broadcast([P, 4, 2, T])
                    o4 = flat(24, 8).rearrange("p (h v t) -> p h v t", h=4, v=2)
                    step(TT(o4, o4, rg, ALU.mult))
                    for c in range(NC):
                        at = GAIN_AT["gla_gn"] + c
                        ins = STT(units(16 + c)[:, 0, :], units(24 + c)[:, 0, :], gain[:, at:at + 1],
                                  units(16 + c)[:, 0, :], ALU.mult, ALU.mult)
                    done("og", ins)

            def attend(name, ng, dst):
                n0 = ng * P
                pe_did(v, f"{name}.qk")
                vec.tensor_reduce(stat[:, 0:1], misc[:, 0, 0:n0], AX_X, ALU.max)
                step(vec.tensor_reduce(stat[:, 1:2], misc_flat[:, 512:512 + 2 * n0], AX_X, ALU.max))
                done(f"{name}.max", TS(stat[:, 2:4], stat[:, 0:2], -1.0, None, ALU.mult))
                ac_did(v, f"{name}.exp")
                step(vec.reciprocal(stat[:, 0:2], stat[:, 4:6]))
                TS(logit[:, 0:n0], logit[:, 0:n0], stat[:, 0:1], None, ALU.mult)
                done(f"{name}.norm", TS(logit[:, n0:3 * n0], logit[:, n0:3 * n0], stat[:, 1:2], None, ALU.mult))
                pe_did(v, f"{name}.pv")
                done(f"{name}.o", vec.tensor_copy(dst, misc[:, 3, 0:T]))

            v.wait_ge(const_ready, 1)
            pe_did(v, "gainT")
            done("gain", vec.tensor_copy(gain[:, :], ps[:, 0, 0, 0:GAIN_N]))
            pe_did(v, "tapsT")
            done("taps", vec.tensor_copy(taps[:, :, :], ps[:, 0, 1, 0:256].rearrange("p (c j) -> p c j", c=NC)
                                         [:, :, 0:CONV_W]))
            pe_did(v, "rel")
            vec.tensor_copy(relout[:, 0:BIAS_N], ps[0:ATT_H, 1, 0, 0:BIAS_N])
            vec.tensor_copy(relout[:, BIAS_N:2 * BIAS_N], ps[0:ATT_H, 1, 1, 0:BIAS_N])
            done("rel", vec.tensor_copy(relout[:, 2 * BIAS_N:3 * BIAS_N], misc[0:ATT_H, 3, 0:BIAS_N]))
            for c in range(4):
                pe_did(v, f"xT{c}")
                vec.tensor_copy(x[:, 2 * c:2 * c + 2, :], misc[:, c, :].rearrange("p (k t) -> p k t", k=2)
                                ).then_inc(new_x, 1)
                v.wait_ge(new_x, c + 1)
                split_gained(xa[:, 2 * c:2 * c + 2, :, :], x[:, 2 * c:2 * c + 2, :], GAIN_AT["ln1"] + 2 * c, 2)
                if c == 0:
                    for s in range(3):
                        rest_block(*locate(s), s, None)
            for s in range(3, AHEAD):
                rest_block(*locate(s), s, None)
            ang, turn = val[:, 0, :], val[:, 1, :]
            v.wait_ge(s_setup, 16 * 6)
            step(vec.tensor_copy(ang, posi))
            step(TS(ang, ang, ropec[:, 0:1], None, ALU.mult))
            step(TS(turn, ang, 1.0 / TWO_PI, MAGIC, ALU.mult, ALU.add))
            step(TS(turn, turn, MAGIC, None, ALU.subtract))
            step(STT(ang, turn, -PI_A, ang, ALU.mult, ALU.add))
            step(STT(ang, turn, -PI_B, ang, ALU.mult, ALU.add))
            step(STT(root[:, :], turn, -PI_C, ang, ALU.mult, ALU.add))
            done("trig", STT(rstd[:, :], root[:, :], -1.0, root[:, :], ALU.mult, ALU.max))
            ac_did(v, "trig")
            step(STT(turn, sin[:, :], 2.0, cos[:, :], ALU.mult, ALU.mult))
            step(TT(ang, sin[:, :], sin[:, :], ALU.mult))
            step(TS(cos[:, :], ang, -2.0, 1.0, ALU.mult, ALU.add))
            done("setup", vec.tensor_copy(sin[:, :], turn))

            for p in phases:
                if p.name == "y_gla":
                    split(parts[:, 12:20, :, :], units(16, 8), 8)
                    split(parts[:, 20:24, :, :], units(60, 4), 4)
                if p.name == "pw1":
                    v.wait_ge(used, p.block0)
                    step(vec.memset(upad[:, :, 0:CONV_W - 1], 0.0))
                for groups, turns in p.segments():
                    if turns is not None:
                        base = mine[0]
                        per_turn = {"relu2": 3 * 4, "swiglu": 3 * 2}[p.evac[0]]
                        with v.Fori(0, turns) as i:
                            loop[:] = [i, per_turn]
                            for g in groups:
                                for j in range(len(p.kns)):
                                    ahead(p, g, j, i)
                                evacuate(p, g, i, len(groups))
                        assert mine[0] - base == per_turn, (mine[0] - base, per_turn)
                        mine[0] = base + per_turn * turns
                        loop[:] = [None, 0]
                        continue
                    for g in groups:
                        for j in range(len(p.kns)):
                            ahead(p, g, j, None)
                        if g == 0 and p.name in norm_at:
                            norm_step(norm_at[p.name], token=p.name == "ha")
                        if p.name == "w_pg" and g == 2:
                            pe_did(v, "pT")
                            done("ple_free", vec.tensor_copy(units(44, 2), misc[:, 0, :].rearrange(
                                "p (k t) -> p k t", k=2)))
                            split(parts[:, 16:18, :, :], units(44, 2), 2)
                        evacuate(p, g, None, 0)
                        if p.name == "hr":
                            gla_step(g)
                        if p.name == "gates" and g % 2 == 1:
                            h = g // 2
                            attend(f"att{h}", ATT_G, plain[:, 60 + h, :])
                if p.name == "hr":
                    gla_step(4)
                    gla_step(5)
                if p.name == "w_pp":
                    norm_step("ln_f")
                    for c in range(4):
                        xs = x[:, 2 * c:2 * c + 2, :]
                        step(TT(t2[:, :, :], xs, bcast(rstd[:, :], 2), ALU.mult))
                        at = GAIN_AT["ln_f"] + 2 * c
                        TS(x[:, 2 * c, :], t2[:, 0, :], gain[:, at:at + 1], None, ALU.mult)
                        TS(x[:, 2 * c + 1, :], t2[:, 1, :], gain[:, at + 1:at + 2], None, ALU.mult
                           ).then_inc(new_x, 1)
                        v.wait_ge(new_x, pairs["ffn1_up0"][0] + c + 1)
                        split_gained(xa[:, 2 * c:2 * c + 2, :, :], xs, GAIN_AT["ffn_norm1_2"] + 2 * c, 2)
                    done("lnf", vec.tensor_copy(stat[:, 6:7], consts[:, 0:1]))
                if p.name == "pw1":
                    for c in range(NC):
                        o = plain[:, 10 + c, :]
                        step(TS(o, upad[:, c, 0:T], taps[:, c, 0:1], None, ALU.mult))
                        for j in range(1, CONV_W):
                            ins = STT(o, upad[:, c, j:j + T], taps[:, c, j:j + 1], o, ALU.mult, ALU.add)
                            if j < CONV_W - 1:
                                step(ins)
                        if c % 2:
                            ins.then_inc(new_x, 1)
                            v.wait_ge(new_x, pairs["conv"][0] + c // 2 + 1)
                        else:
                            step(ins)
                    done("conv", vec.tensor_copy(stat[:, 6:7], consts[:, 0:1]))
                    norm_step("conv")
                    for c in range(NC):
                        at = GAIN_AT["conv_norm_2"] + c
                        ins = STT(plain[:, 10 + c, :], plain[:, 10 + c, :], gain[:, at:at + 1], rstd[:, :],
                                  ALU.mult, ALU.mult)
                    done("convn", ins)
                    ac_did(v, "conv")
                    split(parts[:, 16:24, :, :], units(10, 8), 8)
                if p.name == "mla_kr":
                    norm_step("cq")
                    split_gained(parts[:, 4:8, :, :], units(0, 4), GAIN_AT["mla_q_norm_2"], 4)
                    done("cqn", vec.tensor_copy(stat[:, 6:7], consts[:, 0:1]))
                    norm_step("ckv", rstd2, token=True)
                    split_gained(parts[:, 8:10, :, :], units(4, 2), GAIN_AT["mla_kv_norm_2"], 2)
                    done("ckvn", vec.tensor_copy(stat[:, 6:7], consts[:, 0:1]))
                if p.name == "ukv_v":
                    for n in range(2):
                        pe_did(v, f"rope_q{n}")
                        q = units(28 + 2 * n, 2)
                        step(TT(t1[:, :, :], misc[:, n, :].rearrange("p (k t) -> p k t", k=2), bcast(sin[:, :], 2),
                                ALU.mult))
                        step(TT(q, q, bcast(cos[:, :], 2), ALU.mult))
                        ins = TT(q, q, t1[:, :, :], ALU.add)
                        if n == 0:
                            step(ins)
                    done("rope_q", ins)
                    pe_did(v, "rope_k")
                    step(TT(t1[:, 0, :], misc[:, 2, 0:T], sin[:, :], ALU.mult))
                    step(TT(plain[:, 6, :], plain[:, 6, :], cos[:, :], ALU.mult))
                    step(vec.memset(sbias[:, 0, 0, :], 0.0))
                    step(vec.memset(sbias[P - MLA_CHUNK:P, 0, 0, P + MLA_CHUNK:T], NEG))
                    done("rope_k", TT(plain[:, 6, :], plain[:, 6, :], t1[:, 0, :], ALU.add))
                    for h in range(MLA_H):
                        attend(f"mla{h}", 1, plain[:, 48 + h, :])
                    split(parts[:, 0:8, :, :], units(48, 8), 8)
            norm_step("final")
            for c in range(NC):
                at = GAIN_AT["final_norm_2"] + c
                ins = STT(plain[:, 8 + c, :], x[:, c, :], gain[:, at:at + 1], rstd[:, :], ALU.mult, ALU.mult)
            done("final", ins)
            pe_did(v, "outT")
            done("out", vec.tensor_copy(flat(0, 8), misc_flat[:, :]))

        @block.gpsimd
        def _(pl):
            gp = nc.gpsimd
            mine = [0]

            def step(ins):
                mine[0] += 1
                ins.then_inc(pool, 1)
                pl.wait_ge(pool, mine[0])

            step(gp.memset(ident[:, :], 0.0))
            step(gp.affine_select(out=ident[:, :], in_=ident[:, :], compare_op=ALU.not_equal, fill=1.0, base=0,
                                  pattern=[[-1, P]], channel_multiplier=1))
            step(gp.memset(flip[:, :], 0.0))
            step(gp.affine_select(out=flip[:, :], in_=flip[:, :], compare_op=ALU.not_equal, fill=1.0,
                                  base=1 - P, pattern=[[1, P]], channel_multiplier=1))
            step(gp.memset(relrow[REL_BUCKETS:REL_BUCKETS + 1, :], 1.0))
            step(gp.memset(consts[:, 0:1], EPS))
            step(gp.memset(consts[:, 1:2], TWO_PI / 4))
            step(gp.memset(ha, 1.0))
            step(gp.memset(tri[:, :], 1.0 / 16.0))
            step(gp.affine_select(out=tri[:, :], in_=tri[:, :], compare_op=ALU.is_ge, fill=0.0, base=0,
                                  pattern=[[1, P]], channel_multiplier=-1))
            step(gp.memset(tri[0:GLA_CHUNK, GLA_CHUNK:P], 0.0))
            gp.memset(ones[:, :], 1.0).then_inc(const_ready, 1)
            for name, (q0, n) in pairs.items():
                if name == "mlp1":
                    dv_did(pl, "rel")
                    pl.dma_start(bias_dram.rearrange("g h j -> h g j"), relout.rearrange("h (g j) -> h g j", g=ATT_G)
                                 ).then_inc(s_rel, 16)
                    pl.wait_ge(s_rel, 16)
                    pe_did(pl, "z")
                    for h in range(ATT_H):
                        if h >= 2:
                            dv_did(pl, f"att{h - 2}.max")
                        src = bass.AP(bias_dram.tensor, h * BIAS_N,
                                      [[1, P], [ATT_H * BIAS_N, ATT_G], [1, T]])
                        pl.dma_start(sbias[:, h % 2, :, :], src).then_inc(s_bias[h % 2], 16)
                if name == "ln_f":
                    pl.wait_ge(used, by["w_pg"].block0)
                    pl.dma_start(plain[:, 40:42, :], a["p"][0, 0].rearrange("(t p) n -> p t n", p=P)
                                 ).then_inc(s_p, 16)
                if norms[name] >= 1:
                    pl.wait_ge(norm_sum, norms[name])
                for c in range(n):
                    q = q0 + c
                    pl.wait_ge(squared, q + 1)
                    if c == 0:
                        gp.tensor_copy(acc[:, :, :], sq[:, q % 2, :, :]).then_inc(summed, 1)
                    else:
                        pl.wait_ge(summed, q)
                        gp.tensor_tensor(acc[:, :, :], acc[:, :, :], sq[:, q % 2, :, :], ALU.add).then_inc(summed, 1)


TWO_PI = 6.283185307179586
MAGIC = 12582912.0
PI_A = 6.28125
PI_B = float(np.float32(round((TWO_PI - PI_A) * 2 ** 18) / 2 ** 18))
PI_C = float(np.float32(TWO_PI - PI_A - PI_B))

_INS = ["x", "p", "ln1", "w_in", "w_a2", "b_a", "gla_gn", "w_o_gla", "w_o_attn", "w_out", "ln2", "w_mlp1", "w_mlp2",
        "ln3", "w_pp", "w_pg", "rel_bias", "ln_f", "positions_2", "ffn_norm1_2", "ffn1_w1_2", "ffn1_w3_2",
        "ffn1_w2_2", "mix_norm_2", "ffn_norm2_2", "ffn2_w1_2", "ffn2_w3_2", "ffn2_w2_2", "conv_w_pw1_2",
        "conv_w_dw_2", "conv_norm_2", "conv_w_pw2_2", "mla_w_a_2", "mla_q_norm_2", "mla_kv_norm_2", "mla_w_uq_2",
        "mla_w_ukv_2", "mla_w_o_2", "final_norm_2"]


def kernel(**inputs):
    import numpy as _np
    import concourse.bacc as _bacc
    from concourse import mybir as _mybir
    from concourse.bass_utils import run_bass_kernel_spmd as _run

    nc = _bacc.Bacc("TRN2", target_bir_lowering=False, num_devices=1)
    arrays, args = {}, {}
    given = {name: _np.ascontiguousarray(inputs[name]) for name in _INS}
    given["bias_c"] = bias_table()
    given["rope_c"] = rope_table()
    for name, arr in given.items():
        arrays[f"in_{name}_dram"] = arr
        args[name] = nc.dram_tensor(f"in_{name}_dram", arr.shape, _mybir.dt.from_np(arr.dtype),
                                    kind="ExternalInput").ap()
    out = nc.dram_tensor("out_0_dram", (1, T, D), _mybir.dt.float32, kind="ExternalOutput").ap()
    program(nc, args, out)
    r = _run(nc, [arrays], core_ids=[0])
    return r.results[0]["out_0_dram"]
```

```python
from contextlib import ExitStack

import numpy as np

import concourse.bass as bass
from concourse import mybir

F32 = mybir.dt.float32
F32R = mybir.dt.float32r
I32 = mybir.dt.int32
ACT = mybir.ActivationFunctionType
ALU = mybir.AluOpType
AX_X = mybir.AxisListType.X

P = 128
D = 1024
T = 256
NT = T // P
NC = D // P
EPS = 1e-6
W = 256
RAW = 4
RING = 8
ROUND_AHEAD = 7
REST_AHEAD = 5
PLE = 256
GLA_H, GLA_DK, GLA_DV, GLA_RANK, GLA_CHUNK = 4, 128, 256, 16, 64
GLA_QK, GLA_V = GLA_H * GLA_DK, GLA_H * GLA_DV
ATT_GROUPS = ((128, 1), (512, 4), (2048, 16))
ATT_G, ATT_H, HD = 3, 4, 128
ATT_W = ATT_H * HD
REL_BUCKETS, REL_MAX_DIST = 32, 2048
NEG = -1e30
FF1, FF2 = 4 * D, 2816
CONV_W = 31
MLA_H, NOPE, ROPE, VH, Q_LORA, KV_LORA = 8, 128, 64, 128, 512, 256
MLA_CHUNK = 64
ROPE_THETA = 10000.0
BIAS_N = 384

COL_HA = 2 * GLA_QK + 2 * GLA_V
COL_ATT = COL_HA + GLA_RANK
COL_GATE = COL_ATT + ATT_G * 3 * ATT_W

GAINS = (("ln1", 8), ("ln2", 8), ("ln3", 8), ("gla_gn", 8), ("ln_f", 8), ("ffn_norm1_2", 16),
         ("mix_norm_2", 16), ("ffn_norm2_2", 16), ("conv_norm_2", 8), ("mla_q_norm_2", 4),
         ("mla_kv_norm_2", 2), ("final_norm_2", 8))
GAIN_AT, _n = {}, 0
for _name, _c in GAINS:
    GAIN_AT[_name] = _n
    _n += _c
GAIN_N = _n


def bias_table():
    out = np.zeros((REL_BUCKETS + 1, ATT_G, BIAS_N), np.float32)
    exact = REL_BUCKETS // 2
    for g, (win, dil) in enumerate(ATT_GROUPS):
        for j in range(BIAS_N):
            dist = 255 - j
            if dist < 0 or dist > win or dist % dil:
                out[REL_BUCKETS, g, j] = NEG
                continue
            nf = np.float32(max(dist, 1))
            large = exact + int(np.float32(np.log(nf / np.float32(exact)) / np.float32(np.log(REL_MAX_DIST / exact))
                                           * np.float32(REL_BUCKETS - exact)))
            out[dist if dist < exact else min(large, REL_BUCKETS - 1), g, j] = 1.0
    return out


def rope_table():
    half = ROPE // 2
    freq = (ROPE_THETA ** (-2.0 * np.arange(half) / ROPE)).astype(np.float32)
    out = np.zeros((P, 1 + P), np.float32)
    for m in range(P):
        out[m, 0] = freq[m % half]
        if m % ROPE < half:
            out[m + half, 1 + m] = -1.0
        else:
            out[m - half, 1 + m] = 1.0
    return out


def lin(const, coeff, i):
    return const if i is None or coeff == 0 else i * coeff + const


class Phase:

    def __init__(self, name, src, groups, kns, moving, evac, layout="F", width=W, loop=None):
        self.name, self.src, self.groups, self.kns = name, src, groups, kns
        self.moving, self.evac, self.layout, self.width, self.loop = moving, evac, layout, width, loop
        self.k0 = [sum(kns[:j]) for j in range(len(kns))]

    def segments(self):
        if self.loop is None:
            yield list(range(self.groups)), None
            return
        first, per, turns = self.loop
        yield list(range(first)), None
        yield list(range(first, first + per)), turns
        yield list(range(first + per * turns, self.groups)), None

    def block(self, g, j):
        return self.block0 + g * len(self.kns) + j


def program(nc, a, out):
    with ExitStack() as ctx:
        def sb(name, shape, dt=F32):
            return ctx.enter_context(nc.sbuf_tensor(name, shape, dt))

        def sem(name):
            return ctx.enter_context(nc.semaphore(name))

        guard = nc.sbuf_tensor("plain", [P, 64, T], F32)
        plain = guard.__enter__()
        guard.__exit__(None, None, None)
        parts = sb("parts", [P, 32, 2, T], F32R)
        raw = sb("raw", [P, RAW, 4, W])
        wsplit = sb("wsplit", [P, RING, 4, 2, W], F32R)
        xa = sb("xa", [P, NC, 2, T], F32R)
        x = sb("x", [P, NC, T])
        lohalf = sb("lohalf", [P, 2, 2, T])
        val = sb("val", [P, 2, T])
        t1 = sb("t1", [P, 2, T])
        work = sb("work", [P, 5, T])
        t2, gated = work[:, 0:2, :], work[:, 2:4, :]
        sq = sb("sq", [P, 2, 2, T])
        acc = sb("acc", [P, 2, T])
        root = sb("root", [P, T])
        rstd = sb("rstd", [P, T])
        rstd2 = sb("rstd2", [P, T])
        root_tok = sb("root_tok", [P, NT])
        rstd_tok = sb("rstd_tok", [P, NT])
        ident = sb("ident", [P, P])
        ones = sb("ones", [P, P])
        tri = sb("tri", [P, P])
        flip = sb("flip", [P, P])
        gain = sb("gain", [P, GAIN_N])
        taps = sb("taps", [P, NC, CONV_W])
        ropec = sb("ropec", [P, 1 + P])
        cos = sb("cos", [P, T])
        sin = sb("sin", [P, T])
        consts = sb("consts", [P, 2])
        blast = sb("blast", [P, 16])
        sbias = sb("sbias", [P, 2, ATT_G, T])
        logit = sb("logit", [P, 9 * P])
        probT = work[:, :, :].rearrange("p a b -> p (a b)")[:, 0:9 * P]
        wa2 = sbias[0:GLA_RANK + 1, 1, 0:2, :].rearrange("p a b -> p (a b)")
        ha = sbias[0:32, 1, 2, :]
        stat = sb("stat", [P, 16])
        gain_rows = logit[0:GAIN_N, 0:P]
        dw_rows = logit[0:CONV_W, P:P + D]
        relrow = t1[0:REL_BUCKETS + 1, 0, 0:ATT_G * ATT_H]
        onehot = probT[0:REL_BUCKETS + 1, :]
        posi = t1[:, 1, :].bitcast(I32)
        bias_dram = nc.dram_tensor("bias_rows", (ATT_G, ATT_H, BIAS_N), F32, kind="Internal").ap()

        ps = ctx.enter_context(nc.psum_tensor("ps", [P, 2, 2, 512], F32))
        misc = ctx.enter_context(nc.psum_tensor("misc", [P, 4, 512], F32))
        misc_flat = misc[:, :, :].rearrange("p a b -> p (a b)")

        def diag(c, j):
            n = (c - 5) * CONV_W + j
            if n < 9:
                return logit[:, n * P:(n + 1) * P]
            n -= 9
            return plain[:, 18 + n // 2, (n % 2) * P:(n % 2 + 1) * P]

        def units(u, n=1):
            return plain[:, u:u + n, :]

        def flat(u, n=1):
            return plain[:, u:u + n, :].rearrange("p a b -> p (a b)")

        def bcast(ap, n):
            return ap.unsqueeze(1).to_broadcast([P, n, ap.shape[-1]])

        relout = flat(56, 5)[0:ATT_H, 0:ATT_G * BIAS_N]

        def rows(ap):
            return ap.rearrange("(k p) n -> p k n", p=P)

        def cols(ap, at=0, width=W):
            v = rows(ap)
            return lambda g, k, n: [(0, width, v[:, k:k + n, bass.ds(g * width + at, width)])]

        def pair_cols(a1, a2):
            v = rows(a1), rows(a2)
            return lambda g, k, n: [(0, W, v[g[1]][:, k:k + n, bass.ds(g[0] * W, W)])]

        def wide(ap, at, n):
            v = rows(ap)
            return lambda g, k, m: [(0, n, v[:, k:k + m, at:at + n])]

        def lora(ap, first, size, per_head, heads):
            v = ap.rearrange("(k p) h d -> p k h d", p=P)
            return lambda g, k, n: [(h * size, size, v[:, k:k + n, g * heads + h, first:first + size])
                                    for h in range(heads)]

        w_in = a["w_in"][0]
        K8 = [4, 4]
        K22 = [3, 3, 3, 3, 3, 3, 2, 2]
        K32 = [4] * 8

        def from_xa(k):
            return xa[:, k, :, :]

        def from_parts(c):
            return lambda k: parts[:, c + k, :, :]

        phases = []

        def add(*args, **kw):
            phases.append(Phase(*args, **kw))

        add("ha", wide(w_in, COL_HA, P), 1, K8, from_xa, ("ha",), width=P)
        add("gla_q", cols(w_in, 0), 2, K8, from_xa, ("keep", 0))
        add("gla_k", cols(w_in, GLA_QK), 2, K8, from_xa, ("keep", 4))
        add("gla_v", cols(w_in, 2 * GLA_QK), 4, K8, from_xa, ("keep_tok", 8), layout="T")
        add("hr", cols(w_in, 2 * GLA_QK + GLA_V), 4, K8, from_xa, ("func", ACT.Silu, 16))
        for g in (2, 0, 1):
            at, u = COL_ATT + g * 3 * ATT_W, 24 + 12 * g
            add(f"att_q{g}", cols(w_in, at), 2, K8, from_xa, ("keep", u, float(HD) ** -0.5))
            add(f"att_k{g}", cols(w_in, at + ATT_W), 2, K8, from_xa, ("keep", u + 4))
            add(f"att_v{g}", cols(w_in, at + 2 * ATT_W), 2, K8, from_xa, ("keep_tok", u + 8), layout="T")
        add("gates", cols(w_in, COL_GATE), 8, K8, from_xa, ("func", ACT.Sigmoid, 0))
        add("y_gla", cols(a["w_o_gla"][0]), 4, K8, lambda k: parts[:, (12 if k < 4 else 14) + k, :, :], ("times", 0))
        add("y_att", cols(a["w_o_attn"][0]), 4, [4], from_parts(24), ("mix", 0, 8))
        add("w_out", cols(a["w_out"][0]), 4, K8, lambda k: parts[:, (8 if k < 4 else 24) + k, :, :],
            ("resid", 1.0, GAIN_AT["ln2"]))
        add("mlp1", cols(a["w_mlp1"][0]), 16, K8, from_xa, ("relu2",), loop=(4, 4, 2))
        add("mlp2", cols(a["w_mlp2"][0]), 4, K32, from_parts(0), ("resid", 1.0, GAIN_AT["ln3"]))
        add("w_pg", cols(a["w_pg"][0]), 4, K8, from_xa, ("func", ACT.Sigmoid, 0))
        add("w_pp", cols(a["w_pp"][0]), 4, [2], from_parts(16), ("ple", 0))

        def ffn(w, i, nxt):
            add(f"{w}_up{i}", pair_cols(a[f"{w}_w1_2"][i], a[f"{w}_w3_2"][i]), 2 * FF2 // W, K8, from_xa,
                ("swiglu",), loop=(2, 4, 4))
            add(f"{w}_down{i}", cols(a[f"{w}_w2_2"][i]), 4, K22, from_parts(0), ("resid", 0.5, nxt))

        gn = GAIN_AT
        ffn("ffn1", 0, gn["mix_norm_2"])
        pw1 = a["conv_w_pw1_2"][0]
        add("pw1", pair_cols(pw1[:, D:2 * D], pw1[:, 0:D]), 8, K8, from_xa, ("glu",))
        add("pw2", cols(a["conv_w_pw2_2"][0]), 4, K8, from_parts(16), ("resid", 1.0, gn["ffn_norm2_2"]))
        ffn("ffn2", 0, gn["ffn_norm1_2"] + 8)
        ffn("ffn1", 1, gn["mix_norm_2"] + 8)
        w_a = a["mla_w_a_2"][0]
        add("mla_a", cols(w_a), 3, K8, from_xa, ("keep_sq", 0))
        krows = rows(w_a)[:, :, Q_LORA + KV_LORA:]
        add("mla_kr", lambda g, k, n: [(h * ROPE, ROPE, krows[:, k:k + n, :]) for h in range(2)],
            1, K8, from_xa, ("keep", 6), width=P)
        mla_scale = float(NOPE + ROPE) ** -0.5
        uq, ukv = a["mla_w_uq_2"][0], a["mla_w_ukv_2"][0]
        add("uq_nope", lora(uq, 0, NOPE, NOPE + ROPE, 2), 4, [4], from_parts(4), ("keep", 20, mla_scale))
        add("uq_rope", lora(uq, NOPE, ROPE, NOPE + ROPE, 4), 2, [4], from_parts(4), ("keep", 28, mla_scale))
        add("ukv_nope", lora(ukv, 0, NOPE, NOPE + VH, 2), 4, [2], from_parts(8), ("keep", 32))
        add("ukv_v", lora(ukv, NOPE, VH, NOPE + VH, 2), 4, [2], from_parts(8), ("keep_tok", 40), layout="T")
        add("w_o", cols(a["mla_w_o_2"][0]), 4, K8, from_parts(0), ("resid", 1.0, gn["ffn_norm2_2"] + 8))
        ffn("ffn2", 1, None)

        by = {p.name: p for p in phases}
        blocks, nblk, ngrp, ngate, nkept = [], 0, 0, 0, 0
        GATES = {"func": 1, "swiglu": 0.5, "glu": 0.5}
        for p in phases:
            p.block0, p.group0, p.gate0, p.kept0 = nblk, ngrp, ngate, nkept
            nkept += p.groups if p.evac[0] in ("ha", "keep", "keep_tok") else 0
            nblk += p.groups * len(p.kns)
            ngrp += p.groups
            ngate += int(p.groups * GATES.get(p.evac[0], 0))
            blocks += [(p, g, j) for g in range(p.groups) for j in range(len(p.kns))]
        moving, made = {}, 0
        for name, n in (("w_in", 8), ("ogla", 8), ("oatt", 4), ("mix", 8), ("mlp1", 8), ("mlp2", 32), ("w_pg", 8),
                        ("ple", 2), ("ffn1_up0", 8), ("ffn1_down0", 22), ("pw1", 8), ("conv", 8), ("ffn2_up0", 8),
                        ("ffn2_down0", 22), ("ffn1_up1", 8), ("ffn1_down1", 22), ("mla_a", 8), ("cq", 4),
                        ("ckv", 2), ("omla", 8), ("ffn2_up1", 8), ("ffn2_down1", 22)):
            moving[name] = made
            made += n
        source = {"y_gla": "ogla", "y_att": "oatt", "w_out": "mix", "w_pp": "ple", "pw2": "conv", "mla_kr": "mla_a",
                  "uq_nope": "cq", "uq_rope": "cq", "ukv_nope": "ckv", "ukv_v": "ckv", "w_o": "omla"}
        for p in phases:
            p.ready = moving[source.get(p.name, p.name if p.name in moving else "w_in")]
        after = {"w_out": "mlp1", "mlp2": "w_pg", "pw2": "ffn2_up0", "ffn1_down0": "pw1", "ffn2_down0": "ffn1_up1",
                 "ffn1_down1": "mla_a", "w_o": "ffn2_up1"}
        norms, pairs, sums = {}, {}, 0
        for name, n in (("w_in", 4), ("mlp1", 4), ("w_pg", 4), ("ln_f", 4), ("ffn1_up0", 4), ("pw1", 4), ("conv", 4),
                        ("ffn2_up0", 4), ("ffn1_up1", 4), ("mla_a", 4), ("cq", 2), ("ckv", 1), ("ffn2_up1", 4),
                        ("final", 4)):
            norms[name] = len(norms)
            pairs[name] = (sums, n)
            sums += n
        pair_of = {"w_out": "mlp1", "mlp2": "w_pg", "w_pp": "ln_f", "ffn1_down0": "pw1", "pw2": "ffn2_up0",
                   "ffn2_down0": "ffn1_up1", "ffn1_down1": "mla_a", "w_o": "ffn2_up1", "ffn2_down1": "final"}
        norm_at = {"gla_q": "w_in", "mlp1": "mlp1", "w_pg": "w_pg", "ffn1_up0": "ffn1_up0", "pw1": "pw1",
                   "ffn2_up0": "ffn2_up0", "ffn1_up1": "ffn1_up1", "mla_a": "mla_a", "ffn2_up1": "ffn2_up1",
                   "ha": "w_in"}
        del norm_at["gla_q"]

        upad = flat(0, 9)[:, 0:NC * (T + CONV_W - 1)].rearrange("p (c t) -> p c t", c=NC)

        def softmax_places(ng, par):
            n, at = ng * P, par * 3 * P
            return (logit[:, at:at + n], logit[:, at + n:at + 3 * n], probT[:, at:at + n],
                    probT[:, at + n:at + 3 * n], stat[:, 8 * par:8 * par + 6])

        def logit_banks(ng, par):
            if ng == 1:
                return misc[:, par, 0:P], misc[:, par, P:3 * P]
            return misc[:, 0, 0:ng * P], misc_flat[:, 512:512 + 2 * ng * P]

        def probT_banks(ng, par):
            if ng == 1:
                return misc[:, 2 + par, 0:P], misc[:, 2 + par, P:3 * P]
            return logit_banks(ng, par)

        s_rows = sem("s_rows")
        s_setup = sem("s_setup")
        s_x = sem("s_x")
        s_p = sem("s_p")
        s_rel = sem("s_rel")
        s_bias = [sem(f"s_bias{b}") for b in range(2)]
        s_out = sem("s_out")
        raw_landed = [sem(f"raw_landed{i}") for i in range(RAW)]
        hi_done = sem("hi_done")
        lo_done = sem("lo_done")
        used = sem("used")
        lohalf_done = sem("lohalf_done")
        val_done = sem("val_done")
        ready = sem("ready")
        gate_in = sem("gate_in")
        gate_out = sem("gate_out")
        new_x = sem("new_x")
        squared = sem("squared")
        summed = sem("summed")
        norm_sum = sem("norm_sum")
        norm_root = sem("norm_root")
        norm_read = sem("norm_read")
        kept = sem("kept")
        const_ready = sem("const_ready")
        dve = sem("dve")
        actq = sem("actq")
        pool = sem("pool")
        s_pe = sem("s_pe")
        s_dv = sem("s_dv")
        s_ac = sem("s_ac")

        order = {"pe": {}, "dv": {}, "ac": {}}

        def name_steps(engine, names):
            for n in names:
                order[engine][n] = len(order[engine]) + 1

        def one_ahead(first, others):
            names = [f"mla0.{first}"]
            for h in range(MLA_H):
                names += [f"mla{h + 1}.{first}"] if h + 1 < MLA_H else []
                names += [f"mla{h}.{s}" for s in others]
            return names

        name_steps("pe", ["gainT", "tapsT", "rel"] + [f"xT{c}" for c in range(4)]
                   + ["z", "cum", "scores", "koutT", "upd0", "upd1", "upd2", "o", "osum", "att0.qk"]
                   + [n for h in range(3) for n in (f"att{h}.pT", f"att{h}.pv", f"att{h + 1}.qk")]
                   + ["att3.pT", "att3.pv", "pT", "conv5", "conv6", "conv7", "rope_q0", "rope_q1", "rope_k"]
                   + one_ahead("qk", ("pT", "pv")) + ["outT"])
        mla_dv = ["mla0.max"]
        for h in range(MLA_H):
            mla_dv += [f"mla{h + 1}.max"] if h + 1 < MLA_H else []
            mla_dv += [f"mla{h}.norm"] + ([f"mla{h - 1}.o"] if h else [])
        name_steps("dv", ["gain", "taps", "rel", "trig", "setup", "z", "abs", "log", "b", "blast", "gla_in", "attn"]
                   + ["st0", "st1", "st2", "osq", "og"]
                   + [f"att{h}.{s}" for h in range(ATT_H) for s in ("max", "norm", "o")]
                   + ["ple_free", "lnf", "glu", "conv", "convn", "cqn", "ckvn", "rope_q", "rope_k"]
                   + mla_dv + ["mla7.o", "final", "out"])
        name_steps("ac", ["trig", "log", "expb", "expd", "ktok", "o", "oroot"]
                   + [f"att{h}.{s}" for h in range(ATT_H) for s in ("exp", "pT")]
                   + ["diag5", "diag6", "diag7", "conv"] + one_ahead("exp", ("pT",)))

        def pe_did(e, n):
            e.wait_ge(s_pe, order["pe"][n])

        def dv_did(e, n):
            e.wait_ge(s_dv, order["dv"][n])

        def ac_did(e, n):
            e.wait_ge(s_ac, order["ac"][n])

        def locate(s):
            return blocks[s]

        block = ctx.enter_context(nc.Block())

        @block.sync
        def _(sp):
            at = 0
            for name, n in GAINS:
                v = a[name]
                v = v if len(v.shape) == 1 else v.rearrange("a n -> (a n)")
                sp.dma_start(gain_rows[at:at + n, :], v.rearrange("(c p) -> c p", p=P)).then_inc(s_rows, 16)
                at += n
            sp.dma_start(dw_rows, a["conv_w_dw_2"][0]).then_inc(s_rows, 16)
            sp.dma_start(flat(0, 8).rearrange("p (t n) -> p t n", t=NT),
                         a["x"][0].rearrange("(t p) n -> p t n", p=P)).then_inc(s_x, 16)
            sp.dma_start(ropec[:, :], a["rope_c"]).then_inc(s_setup, 16)
            sp.dma_start(posi, a["positions_2"][0].partition_broadcast(P)).then_inc(s_setup, 16)
            sp.dma_start(onehot, a["bias_c"].rearrange("b g j -> b (g j)")).then_inc(s_setup, 16)
            sp.dma_start(relrow[0:REL_BUCKETS, :], a["rel_bias"]).then_inc(s_setup, 16)
            sp.dma_start(wa2[0:GLA_RANK, :], a["w_a2"][0]).then_inc(s_setup, 16)
            sp.dma_start(wa2[GLA_RANK:GLA_RANK + 1, :], a["b_a"]).then_inc(s_setup, 16)

            def load(p, g, j, s0, i, per):
                if s0 >= RAW:
                    sp.wait_ge(lo_done, lin(s0 - RAW + 1, RING, i))
                kn = p.kns[j]
                if p.evac[0] in ("swiglu", "glu"):
                    where = (lin(g // 2, per // 2, i), g % 2)
                else:
                    where = lin(g, per, i)
                pieces = p.src(where, p.k0[j], kn)
                for c, n, src in pieces:
                    sp.dma_start(raw[:, s0 % RAW, 0:kn, c:c + n], src).then_inc(raw_landed[s0 % RAW], 16)

            for p in phases:
                for groups, turns in p.segments():
                    if turns is None:
                        for g in groups:
                            for j in range(len(p.kns)):
                                load(p, g, j, p.block(g, j), None, 0)
                    else:
                        with sp.Fori(0, turns) as i:
                            for g in groups:
                                for j in range(len(p.kns)):
                                    load(p, g, j, p.block(g, j), i, len(groups))
            dv_did(sp, "out")
            sp.dma_start(out[0].rearrange("(t p) n -> p t n", p=P),
                         flat(0, 8).rearrange("p (t n) -> p t n", t=NT)).then_inc(s_out, 16)
            sp.wait_ge(s_out, 16)

        landed, tally = [], [0] * RAW
        for s, (p, g, j) in enumerate(blocks):
            tally[s % RAW] += 16 * len(p.src((0, 0) if p.evac[0] in ("swiglu", "glu") else 0, 0, 1))
            landed.append(tally[s % RAW])

        @block.tensor
        def _(pe):
            mm = nc.tensor.matmul

            def product_group(p, g, i, per, first):
                bank = (p.group0 + g) % 2
                if p.group0 + g >= 2:
                    pe.wait_ge(val_done, lin(p.group0 + g - 1, per, i))
                nk = sum(p.kns)
                for j, kn in enumerate(p.kns):
                    s = p.block(g, j)
                    slot = s % RING
                    pe.wait_ge(lo_done, lin(s + 1, RING if i is not None else 0, i))
                    for kk in range(kn):
                        k = p.k0[j] + kk
                        if first:
                            pe.wait_ge(ready, p.ready + k + 1)
                        mov = p.moving(k)
                        wboth = wsplit[:, slot, kk, :, :]
                        for c in range(p.width // P):
                            o = ps[:, bank, c, :]
                            st, en = k == 0, k == nk - 1
                            if p.layout == "F":
                                mm(o, wboth[:, 0, c * P:(c + 1) * P], mov.rearrange("p h t -> p (h t)"),
                                   start=st, stop=False, skip_group_check=True)
                                last = mm(o[:, T:2 * T], wboth[:, 1, c * P:(c + 1) * P], mov[:, 0, :],
                                          start=False, stop=en, skip_group_check=True)
                            else:
                                mm(o, mov[:, 0, c * P:(c + 1) * P], wboth.rearrange("p h n -> p (h n)"),
                                   start=st, stop=False, skip_group_check=True)
                                last = mm(o[:, T:2 * T], mov[:, 1, c * P:(c + 1) * P], wboth[:, 0, :],
                                          start=False, stop=en, skip_group_check=True)
                    last.then_inc(used, 1)

            def norm_sum_step(name, width=2, token=False):
                q, n = pairs[name]
                pe.wait_ge(summed, q + n)
                if norms[name] >= 1:
                    pe.wait_ge(norm_root, norms[name])
                for c in range(2):
                    last = mm(misc[:, 3, 0:T], ones[:, :], acc[:, c, :], start=(c == 0), stop=(c == 1),
                              skip_group_check=True)
                if token:
                    for t in range(NT):
                        for c in range(2):
                            last = mm(misc[:, 3, T + t:T + t + 1], acc[:, c, t * P:(t + 1) * P], ones[:, 0:1],
                                      start=False, stop=(c == 1), skip_group_check=True)
                last.then_inc(norm_sum, 1)

            def transpose_to(dst, src, n=P):
                return nc.tensor.transpose(dst, src, ident[0:n, 0:n])

            pe.wait_ge(const_ready, 1)
            pe.wait_ge(s_rows, 16 * (len(GAINS) + 1))
            transpose_to(ps[:, 0, 0, 0:GAIN_N], gain_rows, GAIN_N).then_inc(s_pe, 1)
            for c in range(NC):
                last = transpose_to(ps[:, 0, 1, c * 32:c * 32 + CONV_W], dw_rows[:, c * P:(c + 1) * P], CONV_W)
            last.then_inc(s_pe, 1)
            pe.wait_ge(s_setup, 16 * 6)
            for g in range(ATT_G):
                last = mm(ps[0:ATT_H, 1, g % 2, 0:BIAS_N] if g < 2 else misc[0:ATT_H, 3, 0:BIAS_N],
                          relrow[:, g * ATT_H:(g + 1) * ATT_H], onehot[:, g * BIAS_N:(g + 1) * BIAS_N],
                          start=True, stop=True)
            last.then_inc(s_pe, 1)
            pe.wait_ge(s_x, 16)
            xrow = flat(0, 8).rearrange("p (t n) -> p t n", t=NT)
            for q in range(4):
                if q == 3:
                    dv_did(pe, "rel")
                for c in range(2):
                    for t in range(NT):
                        k = 2 * q + c
                        last = transpose_to(misc[:, q, c * T + t * P:c * T + (t + 1) * P],
                                            xrow[:, t, k * P:(k + 1) * P])
                last.then_inc(s_pe, 1)

            def gla_step(k):
                if k == 0:
                    pe.wait_ge(kept, 1)
                    for t in range(NT):
                        last = mm(misc[:, t, :], ha[0:GLA_RANK + 1, t * P:(t + 1) * P], wa2,
                                  start=True, stop=True)
                    last.then_inc(s_pe, 1)
                if k == 1:
                    dv_did(pe, "log")
                    for h in range(GLA_H):
                        for t in range(NT):
                            last = mm(misc_flat[:, h * T + t * P:h * T + (t + 1) * P],
                                      flat(32, 4)[:, t * GLA_QK + h * P:t * GLA_QK + (h + 1) * P], tri[:, :],
                                      start=True, stop=True, skip_group_check=True)
                    last.then_inc(s_pe, 1)
                if k == 2:
                    dv_did(pe, "gla_in")
                    for h in range(GLA_H):
                        for t in range(NT):
                            last = mm(misc_flat[:, (h * NT + t) * P:(h * NT + t + 1) * P],
                                      plain[:, 28 + h, t * P:(t + 1) * P], plain[:, h, t * P:(t + 1) * P],
                                      start=True, stop=True, skip_group_check=True)
                    last.then_inc(s_pe, 1)
                    for h in range(GLA_H):
                        for t in range(NT):
                            last = transpose_to(misc_flat[:, 1024 + (h * NT + t) * P:1024 + (h * NT + t + 1) * P],
                                                plain[:, 4 + h, t * P:(t + 1) * P])
                    last.then_inc(s_pe, 1)
                if k == 3:
                    ac_did(pe, "ktok")
                    dv_did(pe, "attn")
                    for n in range(3):
                        if n == 2:
                            dv_did(pe, "st0")
                        t, r = n // 2, (n % 2) * GLA_CHUNK
                        for h in range(GLA_H):
                            at = (n % 2) * 1024 + h * GLA_DV
                            last = mm(misc_flat[:, at:at + GLA_DV],
                                      flat(40, 4)[r:r + GLA_CHUNK, (h * NT + t) * P:(h * NT + t + 1) * P],
                                      plain[r:r + GLA_CHUNK, 8 + 2 * h + t, :],
                                      start=True, stop=True, skip_group_check=True)
                        last.then_inc(s_pe, 1)
                if k == 4:
                    dv_did(pe, "st2")
                    for h in range(GLA_H):
                        for vh in range(2):
                            c = 2 * h + vh
                            o = misc_flat[:, c * T:(c + 1) * T]
                            for t in range(NT):
                                mm(o[:, t * P:(t + 1) * P], plain[:, 8 + 2 * h + t, vh * P:(vh + 1) * P],
                                   flat(44, 4)[:, (h * NT + t) * P:(h * NT + t + 1) * P],
                                   start=(t == 0), stop=False, skip_group_check=True)
                            for n in range(1, 4):
                                last = mm(o[:, n * GLA_CHUNK:(n + 1) * GLA_CHUNK],
                                          plain[:, 52 + (n - 1) * GLA_H + h, vh * P:(vh + 1) * P],
                                          plain[:, h, n * GLA_CHUNK:(n + 1) * GLA_CHUNK],
                                          start=False, stop=(n == 3), skip_group_check=True)
                    last.then_inc(s_pe, 1)
                if k == 5:
                    dv_did(pe, "osq")
                    for h in range(GLA_H):
                        for vh in range(2):
                            last = mm(misc_flat[:, h * T:(h + 1) * T], ones[:, :], plain[:, 32 + 2 * h + vh, :],
                                      start=(vh == 0), stop=(vh == 1), skip_group_check=True)
                    last.then_inc(s_pe, 1)

            def attend(name, step, ng, qk, value, bias, masked=0, par=0):
                l0, l1, p0, p1, _ = softmax_places(ng, par)
                if step == "qk":
                    o0, o1 = logit_banks(ng, par)
                    for g in range(ng):
                        for t, o in ((0, o0[:, g * P:(g + 1) * P]), (1, o1[:, g * T:(g + 1) * T])):
                            terms = qk(g)
                            for n, (q, k) in enumerate(terms):
                                mm(o, q[:, t * P:(t + 1) * P], k[:, 0:(t + 1) * P], start=(n == 0), stop=False,
                                   skip_group_check=True)
                            m = masked * t
                            last = mm(o[:, m:], flip[:, :], bias[:, g, (1 - t) * P + m:T], start=False, stop=True,
                                      skip_group_check=True)
                    last.then_inc(s_pe, 1)
                if step == "pT":
                    dv_did(pe, f"{name}.norm")
                    o0, o1 = probT_banks(ng, par)
                    for o, l, tiles in ((o0, l0, ng), (o1, l1, 2 * ng)):
                        for n in range(tiles):
                            last = transpose_to(o[:, n * P:(n + 1) * P], l[:, n * P:(n + 1) * P])
                    last.then_inc(s_pe, 1)
                if step == "pv":
                    ac_did(pe, f"{name}.pT")
                    o = misc[:, 3, 0:T] if ng > 1 else ps[:, 0, par, 0:T]
                    for g in range(ng):
                        mm(o[:, 0:P], value(g, 0), p0[:, g * P:(g + 1) * P], start=(g == 0), stop=False,
                           skip_group_check=True)
                    for g in range(ng):
                        for t in range(NT):
                            n = 2 * g + t
                            last = mm(o[:, P:T], value(g, t), p1[:, n * P:(n + 1) * P],
                                      start=False, stop=(g == ng - 1 and t == 1), skip_group_check=True)
                    last.then_inc(s_pe, 1)

            def att_head(h, step):
                if step == "qk":
                    pe.wait_ge(s_bias[h % 2], 16 * (h // 2 + 1))
                    if h == 0:
                        pe.wait_ge(kept, by["att_v1"].kept0 + 2)
                        dv_did(pe, "og")
                if step == "pv" and h:
                    dv_did(pe, f"att{h - 1}.o")
                attend(f"att{h}", step, ATT_G, lambda g: [(plain[:, 24 + 12 * g + h, :], plain[:, 28 + 12 * g + h, :])],
                       lambda g, t: plain[:, 32 + 12 * g + 2 * (h // 2) + t, (h % 2) * P:(h % 2) * P + P],
                       sbias[:, h % 2, :, :])

            def mla_head(h, step):
                if step == "qk" and h == 0:
                    dv_did(pe, "rope_k")
                if step == "pv" and h >= 2:
                    dv_did(pe, f"mla{h - 2}.o")
                r = (h % 2) * ROPE
                attend(f"mla{h}", step, 1,
                       lambda g: [(plain[:, 20 + h, :], plain[:, 32 + h, :]),
                                  (plain[r:r + ROPE, 28 + h // 2, :], plain[r:r + ROPE, 6, :])],
                       lambda g, t: plain[:, 40 + 2 * (h // 2) + t, (h % 2) * P:(h % 2) * P + P],
                       sbias[:, 0, 0:1, :], P, h % 2)

            for p in phases:
                for groups, turns in p.segments():
                    if turns is not None:
                        with pe.Fori(0, turns) as i:
                            for g in groups:
                                product_group(p, g, i, len(groups), False)
                        continue
                    for g in groups:
                        product_group(p, g, None, 0, g == 0)
                        if g == 0 and p.name in norm_at:
                            norm_sum_step(norm_at[p.name], token=p.name == "ha")
                        if p.name == "hr":
                            gla_step(g)
                        if (p.name == "gates" and g % 2 == 0 and g) or (p.name == "y_gla" and g == 0):
                            att_head(g // 2 - 1 if g else 3, "pv")
                        if p.name == "gates":
                            att_head(g // 2, "pT" if g % 2 else "qk")
                        if p.name == "w_pg" and g == 2:
                            pe.wait_ge(s_p, 16)
                            for k in range(2):
                                for t in range(NT):
                                    last = transpose_to(misc[:, 0, k * T + t * P:k * T + (t + 1) * P],
                                                        plain[:, 40 + t, k * P:(k + 1) * P])
                            last.then_inc(s_pe, 1)
                if p.name == "hr":
                    gla_step(4)
                if p.name == "att_q2":
                    gla_step(5)
                if p.name == "w_pp":
                    norm_sum_step("ln_f")
                if p.name == "pw1":
                    dv_did(pe, "glu")
                    for c in range(5, NC):
                        ac_did(pe, f"diag{c}")
                        for j in range(CONV_W):
                            last = mm(misc[:, c - 5, 0:T], diag(c, j), upad[:, c, j:j + T],
                                      start=(j == 0), stop=(j == CONV_W - 1), skip_group_check=True)
                        last.then_inc(s_pe, 1)
                    norm_sum_step("conv")
                if p.name == "mla_kr":
                    norm_sum_step("cq")
                    norm_sum_step("ckv", token=True)
                if p.name == "ukv_v":
                    pe.wait_ge(kept, by["ukv_v"].kept0 + 4)
                    for n in range(2):
                        for c in range(2):
                            last = mm(misc[:, n, c * T:(c + 1) * T], ropec[:, 1:1 + P], plain[:, 28 + 2 * n + c, :],
                                      start=(c == 0), stop=(c == 1), skip_group_check=True)
                        last.then_inc(s_pe, 1)
                    mm(misc[:, 2, 0:T], ropec[:, 1:1 + P], plain[:, 6, :], start=True, stop=True).then_inc(s_pe, 1)
                    mla_head(0, "qk")
                    for h in range(MLA_H):
                        if h + 1 < MLA_H:
                            mla_head(h + 1, "qk")
                        mla_head(h, "pT")
                        mla_head(h, "pv")
            norm_sum_step("final")
            dv_did(pe, "final")
            for k in range(NC):
                for t in range(NT):
                    n = k * NT + t
                    last = transpose_to(misc_flat[:, t * D + k * P:t * D + (k + 1) * P],
                                        plain[:, 8 + k, t * P:(t + 1) * P])
            last.then_inc(s_pe, 1)

        @block.scalar
        def _(act):
            act_fn = nc.scalar.activation
            mine = [0]

            def step(ins):
                mine[0] += 1
                ins.then_inc(actq, 1)
                act.wait_ge(actq, mine[0])

            sides = [0]

            def settle():
                sides[0] += 1
                act.wait_ge(s_ac, sides[0])

            def round_block(p, g, j, s0, i):
                slot, kn = s0 % RING, p.kns[j]
                act.wait_ge(raw_landed[s0 % RAW], lin(landed[s0], 16 * RING // RAW, i))
                if s0 >= RING:
                    act.wait_ge(used, lin(s0 - RING + 1, RING, i))
                nc.scalar.copy(wsplit[:, slot, 0:kn, 0, 0:p.width], raw[:, s0 % RAW, 0:kn, 0:p.width]
                               ).then_inc(hi_done, 1)

            def ahead(p, g, j, i):
                s = p.block(g, j) + ROUND_AHEAD
                if i is None:
                    if s < len(blocks):
                        round_block(*locate(s), s, None)
                else:
                    o = g * len(p.kns) + j + ROUND_AHEAD
                    round_block(p, o // len(p.kns), o % len(p.kns), s, i)

            def take_lohalf(p, g, i, per):
                G = p.group0 + g
                nch = p.width // P
                act.wait_ge(used, lin(p.block(g, len(p.kns) - 1) + 1, RING if i is not None else 0, i))
                if G >= 2:
                    act.wait_ge(val_done, lin(G - 1, per, i))
                nc.scalar.copy(lohalf[:, G % 2, 0:nch, :], ps[:, G % 2, 0:nch, T:2 * T]).then_inc(lohalf_done, 1)

            def square_pair(name, c, src):
                q = pairs[name][0] + c
                act.wait_ge(new_x, q + 1)
                if q >= 2:
                    act.wait_ge(summed, q - 1)
                act_fn(sq[:, q % 2, :, :], src, ACT.Square).then_inc(squared, 1)

            def norm_step(name, features=D, token=False):
                n = norms[name]
                act.wait_ge(norm_sum, n + 1)
                if n >= 1:
                    act.wait_ge(norm_read, n)
                last = act_fn(root[:, :], misc[:, 3, 0:T], ACT.Sqrt, bias=consts[:, 0:1], scale=1.0 / features)
                if token:
                    last = act_fn(root_tok[:, :], misc[:, 3, T:T + NT], ACT.Sqrt, bias=consts[:, 0:1],
                                  scale=1.0 / features)
                last.then_inc(norm_root, 1)

            def evacuate(p, g, i, per):
                kind = p.evac[0]
                take_lohalf(p, g, i, per)
                if kind == "func":
                    n = p.gate0 + g
                    act.wait_ge(gate_in, n + 1)
                    act_fn(units(p.evac[2] + 2 * g, 2), t1[:, :, :], p.evac[1]).then_inc(gate_out, 1)
                if kind in ("swiglu", "glu") and g % 2 == 0:
                    n = p.gate0 + g // 2
                    act.wait_ge(gate_in, lin(n + 1, per // 2, i))
                    act_fn(gated[:, :, :], t1[:, :, :], ACT.Silu if kind == "swiglu" else ACT.Sigmoid
                           ).then_inc(gate_out, 1)
                if kind in ("resid", "ple"):
                    square_pair(pair_of[p.name], g, x[:, 2 * g:2 * g + 2, :])
                if kind == "keep_sq":
                    square_pair("cq" if g < 2 else "ckv", g % 2, units(2 * g, 2))

            def gla_step(k):
                if k == 0:
                    dv_did(act, "abs")
                    step(act_fn(flat(28, 4), flat(28, 4), ACT.Exp, scale=-1.0))
                    nc.scalar.activation(flat(28, 4), flat(28, 4), ACT.Ln, bias=1.0).then_inc(s_ac, 1)
                    settle()
                if k == 1:
                    dv_did(act, "b")
                    act_fn(flat(40, 4), flat(36, 4), ACT.Exp)
                    act_fn(flat(44, 4), flat(36, 4), ACT.Exp, scale=-1.0).then_inc(s_ac, 1)
                    settle()
                    dv_did(act, "blast")
                    act_fn(blast[:, :], blast[:, :], ACT.Exp)
                    act_fn(flat(48, 4), flat(48, 4), ACT.Exp).then_inc(s_ac, 1)
                    settle()
                if k == 2:
                    pe_did(act, "koutT")
                    dv_did(act, "gla_in")
                    nc.scalar.copy(flat(40, 4), misc_flat[:, 1024:2048]).then_inc(s_ac, 1)
                    settle()
                if k == 4:
                    pe_did(act, "o")
                    nc.scalar.copy(flat(24, 8), misc_flat[:, :]).then_inc(s_ac, 1)
                    settle()
                if k == 5:
                    pe_did(act, "osum")
                    act_fn(flat(44, 4), misc_flat[:, 0:1024], ACT.Sqrt, bias=consts[:, 0:1], scale=1.0 / GLA_DV
                           ).then_inc(s_ac, 1)
                    settle()

            def attend(name, ng, what, par=0):
                l0, l1, p0, p1, st = softmax_places(ng, par)
                if what == "exp":
                    dv_did(act, f"{name}.max")
                    o0, o1 = logit_banks(ng, par)
                    act_fn(l0, o0, ACT.Exp, bias=st[:, 2:3], accum_out=st[:, 4:5])
                    act_fn(l1, o1, ACT.Exp, bias=st[:, 3:4], accum_out=st[:, 5:6]).then_inc(s_ac, 1)
                    settle()
                if what == "pT":
                    pe_did(act, f"{name}.pT")
                    o0, o1 = probT_banks(ng, par)
                    nc.scalar.copy(p0, o0)
                    nc.scalar.copy(p1, o1).then_inc(s_ac, 1)
                    settle()

            for s in range(ROUND_AHEAD):
                round_block(*locate(s), s, None)
            act.wait_ge(const_ready, 1)
            for c in range(4):
                square_pair("w_in", c, x[:, 2 * c:2 * c + 2, :])
            dv_did(act, "trig")
            act_fn(sin[:, :], root[:, :], ACT.Sin, scale=0.5)
            act_fn(cos[:, :], rstd[:, :], ACT.Sin, scale=-0.5, bias=consts[:, 1:2]).then_inc(s_ac, 1)
            settle()

            for p in phases:
                for groups, turns in p.segments():
                    if turns is not None:
                        with act.Fori(0, turns) as i:
                            for g in groups:
                                for j in range(len(p.kns)):
                                    ahead(p, g, j, i)
                                evacuate(p, g, i, len(groups))
                        continue
                    for g in groups:
                        for j in range(len(p.kns)):
                            ahead(p, g, j, None)
                        if g == 0 and p.name in norm_at:
                            norm_step(norm_at[p.name], token=p.name == "ha")
                        if p.name == "gates" and g % 2 == 1:
                            attend(f"att{g // 2}", ATT_G, "exp")
                        if (p.name == "gates" and g % 2 == 0 and g) or (p.name == "y_gla" and g == 0):
                            attend(f"att{g // 2 - 1 if g else 3}", ATT_G, "pT")
                        evacuate(p, g, None, 0)
                        if p.name == "hr":
                            gla_step(g)
                        if p.name == "pw1" and g in (1, 3, 5):
                            c = 5 + g // 2
                            for j in range(CONV_W):
                                last = act_fn(diag(c, j), ident[:, :], ACT.Copy, scale=taps[:, c, j:j + 1])
                            last.then_inc(s_ac, 1)
                            settle()
                if p.name == "hr":
                    gla_step(4)
                if p.name == "att_q2":
                    gla_step(5)
                if p.name == "w_pp":
                    norm_step("ln_f")
                    for c in range(4):
                        square_pair("ffn1_up0", c, x[:, 2 * c:2 * c + 2, :])
                if p.name == "pw1":
                    for c in range(4):
                        square_pair("conv", c, units(10 + 2 * c, 2))
                    norm_step("conv")
                    dv_did(act, "convn")
                    act_fn(units(10, 8), units(10, 8), ACT.Silu).then_inc(s_ac, 1)
                    settle()
                if p.name == "mla_kr":
                    norm_step("cq", Q_LORA)
                    norm_step("ckv", KV_LORA, token=True)
                if p.name == "ukv_v":
                    attend("mla0", 1, "exp", 0)
                    for h in range(MLA_H):
                        if h + 1 < MLA_H:
                            attend(f"mla{h + 1}", 1, "exp", (h + 1) % 2)
                        attend(f"mla{h}", 1, "pT", h % 2)
            norm_step("final")

        @block.vector
        def _(v):
            vec = nc.vector
            TT, TS, STT = vec.tensor_tensor, vec.tensor_scalar, vec.scalar_tensor_tensor
            mine = [0]
            loop = [None, 0]

            def step(ins):
                mine[0] += 1
                ins.then_inc(dve, 1)
                v.wait_ge(dve, lin(mine[0], loop[1], loop[0]))

            def done(name, ins):
                ins.then_inc(s_dv, 1)
                v.wait_ge(s_dv, order["dv"][name])

            def keep(p, g, ins):
                ins.then_inc(kept, 1)
                v.wait_ge(kept, p.kept0 + g + 1)

            def rest_block(p, g, j, s0, i):
                slot, kn = s0 % RING, p.kns[j]
                v.wait_ge(hi_done, lin(s0 + 1, RING, i))
                TT(wsplit[:, slot, 0:kn, 1, 0:p.width], raw[:, s0 % RAW, 0:kn, 0:p.width],
                   wsplit[:, slot, 0:kn, 0, 0:p.width].bitcast(F32), ALU.subtract).then_inc(lo_done, 1)

            def ahead(p, g, j, i):
                s = p.block(g, j) + REST_AHEAD
                if i is None:
                    if s < len(blocks):
                        rest_block(*locate(s), s, None)
                else:
                    o = g * len(p.kns) + j + REST_AHEAD
                    rest_block(p, o // len(p.kns), o % len(p.kns), s, i)

            def split_gained(dst, src, at, n):
                for c in range(n):
                    ins = TS(dst[:, c, 0, :], src[:, c, :], gain[:, at + c:at + c + 1], None, ALU.mult)
                step(ins)
                for c in range(n):
                    STT(dst[:, c, 1, :], src[:, c, :], gain[:, at + c:at + c + 1], dst[:, c, 0, :].bitcast(F32),
                        ALU.mult, ALU.subtract).then_inc(ready, 1)

            def split(dst, src, n):
                step(vec.tensor_copy(dst[:, :, 0, :], src))
                TT(dst[:, :, 1, :], src, dst[:, :, 0, :].bitcast(F32), ALU.subtract).then_inc(ready, n)

            def norm_step(name, dst=rstd, token=False):
                v.wait_ge(norm_root, norms[name] + 1)
                if token:
                    step(vec.reciprocal(rstd_tok[:, :], root_tok[:, :]))
                vec.reciprocal(dst[:, :], root[:, :]).then_inc(norm_read, 1)
                v.wait_ge(norm_read, norms[name] + 1)

            def total(p, g, i, per, nparts=P):
                G, nch = p.group0 + g, p.width // P
                v.wait_ge(lohalf_done, lin(G + 1, per, i))
                TT(val[0:nparts, 0:nch, :], ps[0:nparts, G % 2, 0:nch, 0:T], lohalf[0:nparts, G % 2, 0:nch, :],
                   ALU.add).then_inc(val_done, 1)
                v.wait_ge(val_done, lin(G + 1, per, i))

            def evacuate(p, g, i, per):
                kind, nch = p.evac[0], p.width // P
                r2 = bcast(rstd[:, :], nch)
                total(p, g, i, per, GLA_RANK if kind == "ha" else P)
                if kind == "ha":
                    keep(p, g, TT(ha[0:GLA_RANK, :], val[0:GLA_RANK, 0, :], rstd[0:GLA_RANK, :], ALU.mult))
                if kind == "keep":
                    r = rstd2 if p.name in ("ukv_nope",) else rstd
                    scale = p.evac[2] if len(p.evac) > 2 else 1.0
                    keep(p, g, STT(units(p.evac[1] + 2 * g, nch), val[:, 0:nch, :], scale, bcast(r[:, :], nch),
                                   ALU.mult, ALU.mult))
                if kind == "keep_sq":
                    name, c = ("cq" if g < 2 else "ckv"), g % 2
                    TT(units(2 * g, 2), val[:, :, :], r2, ALU.mult).then_inc(new_x, 1)
                    v.wait_ge(new_x, pairs[name][0] + c + 1)
                if kind == "keep_tok":
                    for t in range(NT):
                        ins = TS(plain[:, p.evac[1] + 2 * g + t, :], val[:, t, :], rstd_tok[:, t:t + 1], None, ALU.mult)
                    keep(p, g, ins)
                if kind == "func":
                    n = p.gate0 + g
                    if n >= 1:
                        v.wait_ge(gate_out, n)
                    TT(t1[:, :, :], val[:, :, :], r2, ALU.mult).then_inc(gate_in, 1)
                    v.wait_ge(gate_in, n + 1)
                if kind in ("swiglu", "glu") and g % 2 == 0:
                    n = p.gate0 + g // 2
                    v.wait_ge(gate_out, lin(n, per // 2, i))
                    TT(t1[:, :, :], val[:, :, :], r2, ALU.mult).then_inc(gate_in, 1)
                    v.wait_ge(gate_in, lin(n + 1, per // 2, i))
                if kind in ("swiglu", "glu") and g % 2 == 1:
                    n, c = p.gate0 + g // 2, lin(g - 1, per, i)
                    if kind == "glu":
                        step(TT(t2[:, :, :], val[:, :, :], r2, ALU.mult))
                    v.wait_ge(gate_out, lin(n + 1, per // 2, i))
                    if kind == "glu":
                        step(TT(upad[:, g - 1:g + 1, CONV_W - 1:], t2[:, :, :], gated[:, :, :], ALU.mult))
                    else:
                        step(TT(t2[:, :, :], val[:, :, :], gated[:, :, :], ALU.mult))
                        split(parts[:, bass.ds(c, 2), :, :], t2[:, :, :], 2)
                if kind == "relu2":
                    c = lin(2 * g, 2 * per, i)
                    step(STT(t2[:, :, :], val[:, :, :], 0.0, val[:, :, :], ALU.max, ALU.mult))
                    split(parts[:, bass.ds(c, 2), :, :], t2[:, :, :], 2)
                if kind == "times":
                    v.wait_ge(gate_out, by["gates"].gate0 + 8)
                    u = p.evac[1] + 2 * g
                    step(TT(units(u, 2), val[:, :, :], units(u, 2), ALU.mult))
                if kind == "mix":
                    u, w = p.evac[1] + 2 * g, p.evac[2] + 2 * g
                    step(TT(t2[:, :, :], val[:, :, :], units(w, 2), ALU.mult))
                    step(TT(t2[:, :, :], t2[:, :, :], units(u, 2), ALU.add))
                    c = (8 if g < 2 else 24) + 2 * g
                    split(parts[:, c:c + 2, :, :], t2[:, :, :], 2)
                if kind == "resid":
                    xs = x[:, 2 * g:2 * g + 2, :]
                    if p.name == "mlp2" or "_down" in p.name:
                        if g == 0 and p.name == "mlp2":
                            step(TT(rstd[:, :], rstd[:, :], rstd[:, :], ALU.mult))
                        step(TT(val[:, :, :], val[:, :, :], r2, ALU.mult))
                    STT(xs, val[:, :, :], p.evac[1], xs, ALU.mult, ALU.add).then_inc(new_x, 1)
                    v.wait_ge(new_x, pairs[pair_of[p.name]][0] + g + 1)
                    if p.evac[2] is not None:
                        split_gained(xa[:, 2 * g:2 * g + 2, :, :], xs, p.evac[2] + 2 * g, 2)
                if kind == "ple":
                    v.wait_ge(gate_out, by["w_pg"].gate0 + 4)
                    xs = x[:, 2 * g:2 * g + 2, :]
                    step(TT(t2[:, :, :], val[:, :, :], units(2 * g, 2), ALU.mult))
                    TT(xs, xs, t2[:, :, :], ALU.add).then_inc(new_x, 1)
                    v.wait_ge(new_x, pairs[pair_of[p.name]][0] + g + 1)

            def gla_step(k):
                b3 = flat(36, 4).rearrange("p (h c t) -> p h c t", h=GLA_H, c=4)
                if k == 0:
                    pe_did(v, "z")
                    done("z", vec.tensor_copy(flat(24, 4), misc_flat[:, 0:1024]))
                    done("abs", STT(flat(28, 4), flat(24, 4), -1.0, flat(24, 4), ALU.mult, ALU.max))
                    ac_did(v, "log")
                    done("log", STT(flat(32, 4), flat(24, 4), 0.0, flat(28, 4), ALU.min, ALU.subtract))
                if k == 1:
                    pe_did(v, "cum")
                    done("b", vec.tensor_copy(flat(36, 4), misc_flat[:, 0:1024]))
                    bl = b3[:, :, :, GLA_CHUNK - 1:GLA_CHUNK].rearrange("p h c t -> p (h c t)")
                    step(vec.tensor_copy(blast[:, :], bl))
                    done("blast", TT(flat(48, 4).rearrange("p (n t) -> p n t", n=16),
                                     blast[:, :].unsqueeze(2).to_broadcast([P, 16, GLA_CHUNK]),
                                     flat(36, 4).rearrange("p (n t) -> p n t", n=16), ALU.subtract))
                    ac_did(v, "expd")
                    step(STT(flat(0, 4), flat(0, 4), float(GLA_DK) ** -0.5, flat(40, 4), ALU.mult, ALU.mult))
                    step(TT(flat(28, 4), flat(4, 4), flat(44, 4), ALU.mult))
                    done("gla_in", TT(flat(4, 4), flat(4, 4), flat(48, 4), ALU.mult))
                    step(vec.memset(flat(44, 4), 0.0))
                if k == 2:
                    pe_did(v, "scores")
                    done("attn", vec.copy_predicated(
                        flat(44, 4).rearrange("p (n t) -> p n t", n=8), bcast(tri[:, :].bitcast(I32), 8),
                        misc_flat[:, 0:1024].rearrange("p (n t) -> p n t", n=8)))
                if k == 3:
                    pe_did(v, "upd0")
                    v.wait_ge(s_rel, 16)
                    done("st0", vec.tensor_copy(flat(52, 4), misc_flat[:, 0:1024]))
                    for n in (1, 2):
                        pe_did(v, f"upd{n}")
                        for h in range(GLA_H):
                            at = (n % 2) * 1024 + h * GLA_DV
                            ins = STT(plain[:, 52 + n * 4 + h, :], plain[:, 48 + n * 4 + h, :],
                                      blast[:, h * 4 + n:h * 4 + n + 1], misc_flat[:, at:at + GLA_DV],
                                      ALU.mult, ALU.add)
                        done(f"st{n}", ins)
                if k == 4:
                    ac_did(v, "o")
                    done("osq", TT(flat(32, 8), flat(24, 8), flat(24, 8), ALU.mult))
                if k == 5:
                    v.wait_ge(gate_out, by["hr"].gate0 + 4)
                    ac_did(v, "oroot")
                    step(vec.reciprocal(flat(44, 4), flat(44, 4)))
                    rg = plain[:, 44:48, :].unsqueeze(2).to_broadcast([P, 4, 2, T])
                    o4 = flat(24, 8).rearrange("p (h v t) -> p h v t", h=4, v=2)
                    step(TT(o4, o4, rg, ALU.mult))
                    for c in range(NC):
                        at = GAIN_AT["gla_gn"] + c
                        ins = STT(units(16 + c)[:, 0, :], units(24 + c)[:, 0, :], gain[:, at:at + 1],
                                  units(16 + c)[:, 0, :], ALU.mult, ALU.mult)
                    done("og", ins)

            def attend(name, ng, what, dst=None, par=0):
                l0, l1, _, _, st = softmax_places(ng, par)
                if what == "max":
                    pe_did(v, f"{name}.qk")
                    o0, o1 = logit_banks(ng, par)
                    vec.tensor_reduce(st[:, 0:1], o0, AX_X, ALU.max)
                    step(vec.tensor_reduce(st[:, 1:2], o1, AX_X, ALU.max))
                    done(f"{name}.max", TS(st[:, 2:4], st[:, 0:2], -1.0, None, ALU.mult))
                if what == "norm":
                    ac_did(v, f"{name}.exp")
                    step(vec.reciprocal(st[:, 0:2], st[:, 4:6]))
                    TS(l0, l0, st[:, 0:1], None, ALU.mult)
                    done(f"{name}.norm", TS(l1, l1, st[:, 1:2], None, ALU.mult))
                if what == "o":
                    pe_did(v, f"{name}.pv")
                    done(f"{name}.o", vec.tensor_copy(dst, misc[:, 3, 0:T] if ng > 1 else ps[:, 0, par, 0:T]))

            v.wait_ge(const_ready, 1)
            pe_did(v, "gainT")
            done("gain", vec.tensor_copy(gain[:, :], ps[:, 0, 0, 0:GAIN_N]))
            pe_did(v, "tapsT")
            done("taps", vec.tensor_copy(taps[:, :, :], ps[:, 0, 1, 0:256].rearrange("p (c j) -> p c j", c=NC)
                                         [:, :, 0:CONV_W]))
            pe_did(v, "rel")
            vec.tensor_copy(relout[:, 0:BIAS_N], ps[0:ATT_H, 1, 0, 0:BIAS_N])
            vec.tensor_copy(relout[:, BIAS_N:2 * BIAS_N], ps[0:ATT_H, 1, 1, 0:BIAS_N])
            done("rel", vec.tensor_copy(relout[:, 2 * BIAS_N:3 * BIAS_N], misc[0:ATT_H, 3, 0:BIAS_N]))
            for c in range(4):
                pe_did(v, f"xT{c}")
                vec.tensor_copy(x[:, 2 * c:2 * c + 2, :], misc[:, c, :].rearrange("p (k t) -> p k t", k=2)
                                ).then_inc(new_x, 1)
                v.wait_ge(new_x, c + 1)
                split_gained(xa[:, 2 * c:2 * c + 2, :, :], x[:, 2 * c:2 * c + 2, :], GAIN_AT["ln1"] + 2 * c, 2)
                if c == 0:
                    for s in range(3):
                        rest_block(*locate(s), s, None)
            for s in range(3, REST_AHEAD):
                rest_block(*locate(s), s, None)
            ang, turn = val[:, 0, :], val[:, 1, :]
            v.wait_ge(s_setup, 16 * 6)
            step(vec.tensor_copy(ang, posi))
            step(TS(ang, ang, ropec[:, 0:1], None, ALU.mult))
            step(TS(turn, ang, 1.0 / TWO_PI, MAGIC, ALU.mult, ALU.add))
            step(TS(turn, turn, MAGIC, None, ALU.subtract))
            step(STT(ang, turn, -PI_A, ang, ALU.mult, ALU.add))
            step(STT(ang, turn, -PI_B, ang, ALU.mult, ALU.add))
            step(STT(root[:, :], turn, -PI_C, ang, ALU.mult, ALU.add))
            done("trig", STT(rstd[:, :], root[:, :], -1.0, root[:, :], ALU.mult, ALU.max))
            ac_did(v, "trig")
            step(STT(turn, sin[:, :], 2.0, cos[:, :], ALU.mult, ALU.mult))
            step(TT(ang, sin[:, :], sin[:, :], ALU.mult))
            step(TS(cos[:, :], ang, -2.0, 1.0, ALU.mult, ALU.add))
            done("setup", vec.tensor_copy(sin[:, :], turn))

            for p in phases:
                if p.name == "y_gla":
                    split(parts[:, 12:16, :, :], units(16, 4), 4)
                    split(parts[:, 18:22, :, :], units(20, 4), 4)
                if p.name == "pw1":
                    v.wait_ge(used, p.block0)
                    step(vec.memset(upad[:, :, 0:CONV_W - 1], 0.0))
                for groups, turns in p.segments():
                    if turns is not None:
                        base = mine[0]
                        per_turn = {"relu2": 2 * 4, "swiglu": 2 * 2}[p.evac[0]]
                        with v.Fori(0, turns) as i:
                            loop[:] = [i, per_turn]
                            for g in groups:
                                for j in range(len(p.kns)):
                                    ahead(p, g, j, i)
                                evacuate(p, g, i, len(groups))
                        assert mine[0] - base == per_turn, (mine[0] - base, per_turn)
                        mine[0] = base + per_turn * turns
                        loop[:] = [None, 0]
                        continue
                    for g in groups:
                        for j in range(len(p.kns)):
                            ahead(p, g, j, None)
                        if g == 0 and p.name in norm_at:
                            norm_step(norm_at[p.name], token=p.name == "ha")
                        if p.name == "w_pg" and g == 2:
                            pe_did(v, "pT")
                            done("ple_free", vec.tensor_copy(units(44, 2), misc[:, 0, :].rearrange(
                                "p (k t) -> p k t", k=2)))
                            split(parts[:, 16:18, :, :], units(44, 2), 2)
                        if p.name == "gates" and g % 2 == 1:
                            attend(f"att{g // 2}", ATT_G, "max")
                            attend(f"att{g // 2}", ATT_G, "norm")
                        evacuate(p, g, None, 0)
                        if p.name == "hr":
                            gla_step(g)
                        if (p.name == "gates" and g % 2 == 0 and g) or (p.name == "y_gla" and g == 0):
                            h = g // 2 - 1 if g else 3
                            attend(f"att{h}", ATT_G, "o", plain[:, 60 + h, :])
                            if h == 3:
                                split(parts[:, 24:28, :, :], units(60, 4), 4)
                if p.name == "hr":
                    gla_step(4)
                if p.name == "att_q2":
                    gla_step(5)
                if p.name == "w_pp":
                    norm_step("ln_f")
                    for c in range(4):
                        xs = x[:, 2 * c:2 * c + 2, :]
                        step(TT(t2[:, :, :], xs, bcast(rstd[:, :], 2), ALU.mult))
                        at = GAIN_AT["ln_f"] + 2 * c
                        TS(x[:, 2 * c, :], t2[:, 0, :], gain[:, at:at + 1], None, ALU.mult)
                        TS(x[:, 2 * c + 1, :], t2[:, 1, :], gain[:, at + 1:at + 2], None, ALU.mult
                           ).then_inc(new_x, 1)
                        v.wait_ge(new_x, pairs["ffn1_up0"][0] + c + 1)
                        split_gained(xa[:, 2 * c:2 * c + 2, :, :], xs, GAIN_AT["ffn_norm1_2"] + 2 * c, 2)
                    done("lnf", vec.tensor_copy(stat[:, 6:7], consts[:, 0:1]))
                if p.name == "pw1":
                    done("glu", vec.tensor_copy(stat[:, 6:7], consts[:, 0:1]))
                    for some in ((0, 1, 2), (3, 4)):
                        for j in range(CONV_W):
                            for c in some:
                                o = plain[:, 10 + c, :]
                                if j:
                                    v.wait_ge(dve, mine[0] - len(some) + 1)
                                    ins = STT(o, upad[:, c, j:j + T], taps[:, c, j:j + 1], o, ALU.mult, ALU.add)
                                else:
                                    ins = TS(o, upad[:, c, 0:T], taps[:, c, 0:1], None, ALU.mult)
                                mine[0] += 1
                                ins.then_inc(dve, 1)
                        v.wait_ge(dve, mine[0])
                        if some[0] == 0:
                            vec.tensor_copy(stat[:, 8:9], consts[:, 0:1]).then_inc(new_x, 1)
                    pe_did(v, "conv5")
                    vec.tensor_copy(plain[:, 15, :], misc[:, 0, 0:T]).then_inc(new_x, 1)
                    pe_did(v, "conv7")
                    vec.tensor_copy(units(16, 2), misc[:, 1:3, 0:T]).then_inc(new_x, 1)
                    vec.tensor_copy(stat[:, 9:10], consts[:, 0:1]).then_inc(new_x, 1)
                    v.wait_ge(new_x, pairs["conv"][0] + 4)
                    done("conv", vec.tensor_copy(stat[:, 6:7], consts[:, 0:1]))
                    norm_step("conv")
                    for c in range(NC):
                        at = GAIN_AT["conv_norm_2"] + c
                        ins = STT(plain[:, 10 + c, :], plain[:, 10 + c, :], gain[:, at:at + 1], rstd[:, :],
                                  ALU.mult, ALU.mult)
                    done("convn", ins)
                    ac_did(v, "conv")
                    split(parts[:, 16:24, :, :], units(10, 8), 8)
                if p.name == "mla_kr":
                    norm_step("cq")
                    split_gained(parts[:, 4:8, :, :], units(0, 4), GAIN_AT["mla_q_norm_2"], 4)
                    done("cqn", vec.tensor_copy(stat[:, 6:7], consts[:, 0:1]))
                    norm_step("ckv", rstd2, token=True)
                    split_gained(parts[:, 8:10, :, :], units(4, 2), GAIN_AT["mla_kv_norm_2"], 2)
                    done("ckvn", vec.tensor_copy(stat[:, 6:7], consts[:, 0:1]))
                if p.name == "ukv_v":
                    for n in range(2):
                        pe_did(v, f"rope_q{n}")
                        q = units(28 + 2 * n, 2)
                        step(TT(t1[:, :, :], misc[:, n, :].rearrange("p (k t) -> p k t", k=2), bcast(sin[:, :], 2),
                                ALU.mult))
                        step(TT(q, q, bcast(cos[:, :], 2), ALU.mult))
                        ins = TT(q, q, t1[:, :, :], ALU.add)
                        if n == 0:
                            step(ins)
                    done("rope_q", ins)
                    pe_did(v, "rope_k")
                    step(TT(t1[:, 0, :], misc[:, 2, 0:T], sin[:, :], ALU.mult))
                    step(TT(plain[:, 6, :], plain[:, 6, :], cos[:, :], ALU.mult))
                    step(vec.memset(sbias[:, 0, 0, :], 0.0))
                    step(vec.memset(sbias[P - MLA_CHUNK:P, 0, 0, P + MLA_CHUNK:T], NEG))
                    done("rope_k", TT(plain[:, 6, :], plain[:, 6, :], t1[:, 0, :], ALU.add))
                    attend("mla0", 1, "max")
                    for h in range(MLA_H):
                        if h + 1 < MLA_H:
                            attend(f"mla{h + 1}", 1, "max", par=(h + 1) % 2)
                        attend(f"mla{h}", 1, "norm", par=h % 2)
                        if h:
                            attend(f"mla{h - 1}", 1, "o", plain[:, 47 + h, :], (h - 1) % 2)
                    attend("mla7", 1, "o", plain[:, 55, :], 1)
                    split(parts[:, 0:8, :, :], units(48, 8), 8)
            norm_step("final")
            for c in range(NC):
                at = GAIN_AT["final_norm_2"] + c
                ins = STT(plain[:, 8 + c, :], x[:, c, :], gain[:, at:at + 1], rstd[:, :], ALU.mult, ALU.mult)
            done("final", ins)
            pe_did(v, "outT")
            done("out", vec.tensor_copy(flat(0, 8), misc_flat[:, :]))

        @block.gpsimd
        def _(pl):
            gp = nc.gpsimd
            mine = [0]

            def step(ins):
                mine[0] += 1
                ins.then_inc(pool, 1)
                pl.wait_ge(pool, mine[0])

            step(gp.memset(ident[:, :], 0.0))
            step(gp.affine_select(out=ident[:, :], in_=ident[:, :], compare_op=ALU.not_equal, fill=1.0, base=0,
                                  pattern=[[-1, P]], channel_multiplier=1))
            step(gp.memset(flip[:, :], 0.0))
            step(gp.affine_select(out=flip[:, :], in_=flip[:, :], compare_op=ALU.not_equal, fill=1.0,
                                  base=1 - P, pattern=[[1, P]], channel_multiplier=1))
            step(gp.memset(relrow[REL_BUCKETS:REL_BUCKETS + 1, :], 1.0))
            step(gp.memset(consts[:, 0:1], EPS))
            step(gp.memset(consts[:, 1:2], TWO_PI / 4))
            step(gp.memset(ha, 1.0))
            step(gp.memset(tri[:, :], 1.0 / 16.0))
            step(gp.affine_select(out=tri[:, :], in_=tri[:, :], compare_op=ALU.is_ge, fill=0.0, base=0,
                                  pattern=[[1, P]], channel_multiplier=-1))
            step(gp.memset(tri[0:GLA_CHUNK, GLA_CHUNK:P], 0.0))
            gp.memset(ones[:, :], 1.0).then_inc(const_ready, 1)
            for name, (q0, n) in pairs.items():
                if name == "mlp1":
                    dv_did(pl, "rel")
                    pl.dma_start(bias_dram.rearrange("g h j -> h g j"), relout.rearrange("h (g j) -> h g j", g=ATT_G)
                                 ).then_inc(s_rel, 16)
                    pl.wait_ge(s_rel, 16)
                    pe_did(pl, "z")
                    for h in range(ATT_H):
                        if h >= 2:
                            dv_did(pl, f"att{h - 2}.max")
                        src = bass.AP(bias_dram.tensor, h * BIAS_N,
                                      [[1, P], [ATT_H * BIAS_N, ATT_G], [1, T]])
                        pl.dma_start(sbias[:, h % 2, :, :], src).then_inc(s_bias[h % 2], 16)
                if name == "ln_f":
                    pl.wait_ge(used, by["w_pg"].block0)
                    pl.dma_start(plain[:, 40:42, :], a["p"][0, 0].rearrange("(t p) n -> p t n", p=P)
                                 ).then_inc(s_p, 16)
                if norms[name] >= 1:
                    pl.wait_ge(norm_sum, norms[name])
                for c in range(n):
                    q = q0 + c
                    pl.wait_ge(squared, q + 1)
                    if c == 0:
                        gp.tensor_copy(acc[:, :, :], sq[:, q % 2, :, :]).then_inc(summed, 1)
                    else:
                        pl.wait_ge(summed, q)
                        gp.tensor_tensor(acc[:, :, :], acc[:, :, :], sq[:, q % 2, :, :], ALU.add).then_inc(summed, 1)


TWO_PI = 6.283185307179586
MAGIC = 12582912.0
PI_A = 6.28125
PI_B = float(np.float32(round((TWO_PI - PI_A) * 2 ** 18) / 2 ** 18))
PI_C = float(np.float32(TWO_PI - PI_A - PI_B))

_INS = ["x", "p", "ln1", "w_in", "w_a2", "b_a", "gla_gn", "w_o_gla", "w_o_attn", "w_out", "ln2", "w_mlp1", "w_mlp2",
        "ln3", "w_pp", "w_pg", "rel_bias", "ln_f", "positions_2", "ffn_norm1_2", "ffn1_w1_2", "ffn1_w3_2",
        "ffn1_w2_2", "mix_norm_2", "ffn_norm2_2", "ffn2_w1_2", "ffn2_w3_2", "ffn2_w2_2", "conv_w_pw1_2",
        "conv_w_dw_2", "conv_norm_2", "conv_w_pw2_2", "mla_w_a_2", "mla_q_norm_2", "mla_kv_norm_2", "mla_w_uq_2",
        "mla_w_ukv_2", "mla_w_o_2", "final_norm_2"]


def kernel(**inputs):
    import numpy as _np
    import concourse.bacc as _bacc
    from concourse import mybir as _mybir
    from concourse.bass_utils import run_bass_kernel_spmd as _run

    nc = _bacc.Bacc("TRN2", target_bir_lowering=False, num_devices=1)
    arrays, args = {}, {}
    given = {name: _np.ascontiguousarray(inputs[name]) for name in _INS}
    given["bias_c"] = bias_table()
    given["rope_c"] = rope_table()
    for name, arr in given.items():
        arrays[f"in_{name}_dram"] = arr
        args[name] = nc.dram_tensor(f"in_{name}_dram", arr.shape, _mybir.dt.from_np(arr.dtype),
                                    kind="ExternalInput").ap()
    out = nc.dram_tensor("out_0_dram", (1, T, D), _mybir.dt.float32, kind="ExternalOutput").ap()
    program(nc, args, out)
    r = _run(nc, [arrays], core_ids=[0])
    return r.results[0]["out_0_dram"]
```
